# Optimizing a Trainium2 kernel written in Bass

```python
import math
import jax, jax.numpy as jnp
from jax import lax
import numpy as np

D_MODEL = 2048
BATCH = 1
SEQ = 256
DEPTH = 1

CHUNK = 64
Q_BLOCK = 128
FOX_HEADS = 8
FOX_HEAD_DIM = 128
DIFF_HEADS = 8
DIFF_QK_DIM = 64
DIFF_HEAD_DIM = 2 * DIFF_QK_DIM
ROPE_DIM = DIFF_QK_DIM // 4
ROPE_THETA = 500000.0
D_FF = 5504
CONV_WIDTH = 3
EPS = 1e-6
NEG_INF = -1e30
FOX_W = FOX_HEADS * FOX_HEAD_DIM
DIFF_W = DIFF_HEADS * DIFF_HEAD_DIM
MIX_W = FOX_W + DIFF_W
IN_COLS = 3 * FOX_W + FOX_HEADS + 3 * DIFF_W

kernel_name = "hybrid_fox_diffattn_convffn"

def rms_norm(x, g):
    xf = x.astype(jnp.float32)
    y = xf * lax.rsqrt(jnp.mean(xf * xf, axis=-1, keepdims=True) + EPS)
    return (y * g.astype(jnp.float32)).astype(x.dtype)

def partial_rope(x, cos, sin):
    half = ROPE_DIM // 2
    xr, xp = x[..., :ROPE_DIM], x[..., ROPE_DIM:]
    x1, x2 = xr[..., :half], xr[..., half:]
    c = cos[None, :, None, None, :].astype(x.dtype)
    s = sin[None, :, None, None, :].astype(x.dtype)
    rot = jnp.concatenate([x1 * c - x2 * s, x2 * c + x1 * s], axis=-1)
    return jnp.concatenate([rot, xp], axis=-1)

def mixer_layer(x, norm1_g, w_in, b_forget, fox_q_g, fox_k_g, diff_q_g, diff_k_g,
                lam_q1, lam_k1, lam_q2, lam_k2, diff_subln_g, w_out, layer_idx):
    B, S, _ = x.shape
    nb = S // Q_BLOCK
    lambda_init = 0.8 - 0.6 * math.exp(-0.3 * layer_idx)
    h = rms_norm(x, norm1_g)
    proj = h @ w_in
    cuts = [FOX_W, 2 * FOX_W, 3 * FOX_W, 3 * FOX_W + FOX_HEADS,
            3 * FOX_W + FOX_HEADS + DIFF_W, 3 * FOX_W + FOX_HEADS + 2 * DIFF_W]
    fq, fk, fv, flog, dq, dk, dv = jnp.split(proj, cuts, axis=-1)

    pos = jnp.arange(S, dtype=jnp.int32)

    fq = rms_norm(fq.reshape(B, S, FOX_HEADS, FOX_HEAD_DIM), fox_q_g)
    fk = rms_norm(fk.reshape(B, S, FOX_HEADS, FOX_HEAD_DIM), fox_k_g)
    fv = fv.reshape(B, S, FOX_HEADS, FOX_HEAD_DIM)
    log_f = jax.nn.log_sigmoid(flog.astype(jnp.float32) + b_forget.astype(jnp.float32))
    c = jnp.cumsum(log_f, axis=1)
    fq_blk = fq.reshape(B, nb, Q_BLOCK, FOX_HEADS, FOX_HEAD_DIM).transpose(1, 0, 3, 2, 4)
    cq_blk = c.reshape(B, nb, Q_BLOCK, FOX_HEADS).transpose(1, 0, 3, 2)
    fk_h = fk.transpose(0, 2, 1, 3)
    fv_h = fv.transpose(0, 2, 1, 3)
    ck = c.transpose(0, 2, 1)

    inv_freq = ROPE_THETA ** (-jnp.arange(0, ROPE_DIM, 2, dtype=jnp.float32) / ROPE_DIM)
    ang = pos.astype(jnp.float32)[:, None] * inv_freq[None, :]
    cos, sin = jnp.cos(ang), jnp.sin(ang)
    dq = partial_rope(rms_norm(dq.reshape(B, S, DIFF_HEADS, 2, DIFF_QK_DIM), diff_q_g), cos, sin)
    dk = partial_rope(rms_norm(dk.reshape(B, S, DIFF_HEADS, 2, DIFF_QK_DIM), diff_k_g), cos, sin)
    dv_h = dv.reshape(B, S, DIFF_HEADS, DIFF_HEAD_DIM).transpose(0, 2, 1, 3)
    dq_blk = dq.reshape(B, nb, Q_BLOCK, DIFF_HEADS, 2, DIFF_QK_DIM).transpose(1, 0, 3, 4, 2, 5)
    dk_h = dk.transpose(0, 2, 3, 1, 4)
    lam = (jnp.exp(jnp.sum(lam_q1.astype(jnp.float32) * lam_k1.astype(jnp.float32)))
           - jnp.exp(jnp.sum(lam_q2.astype(jnp.float32) * lam_k2.astype(jnp.float32)))
           + lambda_init)

    qpos_blk = pos.reshape(nb, Q_BLOCK)
    fox_scale = FOX_HEAD_DIM ** -0.5
    diff_scale = DIFF_QK_DIM ** -0.5

    def attend_block(args):
        fq_b, cq_b, dq_b, qpos = args
        s_f = jnp.einsum('bhqd,bhkd->bhqk', fq_b, fk_h).astype(jnp.float32) * fox_scale
        s_f = s_f + cq_b[..., :, None] - ck[..., None, :]
        frame_mask = pos[None, :] <= qpos[:, None]
        p_f = jax.nn.softmax(jnp.where(frame_mask, s_f, NEG_INF), axis=-1)
        o_f = jnp.einsum('bhqk,bhkd->bhqd', p_f.astype(fv_h.dtype), fv_h)
        s_d = jnp.einsum('bhcqd,bhckd->bhcqk', dq_b, dk_h).astype(jnp.float32) * diff_scale
        chunk_mask = (pos[None, :] // CHUNK) <= (qpos[:, None] // CHUNK)
        p_d = jax.nn.softmax(jnp.where(chunk_mask, s_d, NEG_INF), axis=-1)
        a_d = p_d[:, :, 0] - lam * p_d[:, :, 1]
        o_d = jnp.einsum('bhqk,bhkd->bhqd', a_d.astype(dv_h.dtype), dv_h)
        o_d = rms_norm(o_d, diff_subln_g) * (1.0 - lambda_init)
        return o_f, o_d

    o_f, o_d = lax.map(attend_block, (fq_blk, cq_blk, dq_blk, qpos_blk))
    o_f = o_f.transpose(1, 0, 3, 2, 4).reshape(B, S, FOX_W)
    o_d = o_d.transpose(1, 0, 3, 2, 4).reshape(B, S, DIFF_W)
    mixed = jnp.concatenate([o_f, o_d], axis=-1)
    return x + mixed @ w_out

def conv_ffn(x, norm2_g, w_up, conv_w, conv_b, w_down):
    h = rms_norm(x, norm2_g)
    u = h @ w_up
    u = lax.conv_general_dilated(
        u, conv_w[:, None, :].astype(u.dtype), window_strides=(1,),
        padding=[(CONV_WIDTH - 1, 0)], dimension_numbers=('NWC', 'WIO', 'NWC'),
        feature_group_count=2 * D_FF) + conv_b
    gate, val = jnp.split(u, 2, axis=-1)
    return x + (jax.nn.silu(gate) * val) @ w_down

def setup_inputs(seed: int = 0) -> dict:
    key = jax.random.key(seed)
    ks = jax.random.split(key, 20)
    f32 = jnp.float32
    nrm = lambda k, shape, s: jax.random.normal(k, shape, f32) * s
    gain = lambda k, shape: 1.0 + 0.02 * jax.random.normal(k, shape, f32)
    return {
        "x": jax.random.normal(ks[0], (BATCH, SEQ, D_MODEL), f32),
        "norm1_g": gain(ks[1], (DEPTH, D_MODEL)),
        "w_in": nrm(ks[2], (DEPTH, D_MODEL, IN_COLS), D_MODEL ** -0.5),
        "b_forget": 3.0 + 0.5 * jax.random.normal(ks[3], (DEPTH, FOX_HEADS), f32),
        "fox_q_g": gain(ks[4], (DEPTH, FOX_HEAD_DIM)),
        "fox_k_g": gain(ks[5], (DEPTH, FOX_HEAD_DIM)),
        "diff_q_g": gain(ks[6], (DEPTH, DIFF_QK_DIM)),
        "diff_k_g": gain(ks[7], (DEPTH, DIFF_QK_DIM)),
        "lam_q1": nrm(ks[8], (DEPTH, DIFF_QK_DIM), 0.1),
        "lam_k1": nrm(ks[9], (DEPTH, DIFF_QK_DIM), 0.1),
        "lam_q2": nrm(ks[10], (DEPTH, DIFF_QK_DIM), 0.1),
        "lam_k2": nrm(ks[11], (DEPTH, DIFF_QK_DIM), 0.1),
        "diff_subln_g": gain(ks[12], (DEPTH, DIFF_HEAD_DIM)),
        "w_out": nrm(ks[13], (DEPTH, MIX_W, D_MODEL), MIX_W ** -0.5),
        "norm2_g": gain(ks[14], (DEPTH, D_MODEL)),
        "w_up": nrm(ks[15], (DEPTH, D_MODEL, 2 * D_FF), D_MODEL ** -0.5),
        "conv_w": nrm(ks[16], (DEPTH, CONV_WIDTH, 2 * D_FF), CONV_WIDTH ** -0.5),
        "conv_b": nrm(ks[17], (DEPTH, 2 * D_FF), 0.02),
        "w_down": nrm(ks[18], (DEPTH, D_FF, D_MODEL), D_FF ** -0.5),
    }

def reference(x, norm1_g, w_in, b_forget, fox_q_g, fox_k_g, diff_q_g, diff_k_g,
              lam_q1, lam_k1, lam_q2, lam_k2, diff_subln_g, w_out, norm2_g,
              w_up, conv_w, conv_b, w_down):
    for l in range(DEPTH):
        x = mixer_layer(x, norm1_g[l], w_in[l], b_forget[l], fox_q_g[l], fox_k_g[l],
                        diff_q_g[l], diff_k_g[l], lam_q1[l], lam_k1[l], lam_q2[l],
                        lam_k2[l], diff_subln_g[l], w_out[l], l)
        x = conv_ffn(x, norm2_g[l], w_up[l], conv_w[l], conv_b[l], w_down[l])
    return x


_drawn_inputs = setup_inputs


def setup_inputs(seed=0):
    import zlib

    import numpy as np

    out = dict(_drawn_inputs(seed))
    spreads = {}
    factors = {'norm1_g': 2.754,
     'fox_q_g': 8.0,
     'fox_k_g': 8.0,
     'diff_q_g': 4.749,
     'diff_k_g': 5.14,
     'lam_k1': 8.0,
     'lam_q2': 8.0,
     'diff_subln_g': 5.8,
     'norm2_g': 4.179,
     'conv_b': 4.385}
    for name, (base, spread) in spreads.items():
        noise = np.random.default_rng([zlib.crc32(name.encode()), seed]).standard_normal(out[name].shape)
        drawn = base * np.exp(spread * noise) if base else spread * noise
        out[name] = __import__('jax').numpy.asarray(drawn.astype(out[name].dtype))
    for name, factor in factors.items():
        out[name] = (out[name] * factor).astype(out[name].dtype)
    return out
```

```python
from contextlib import ExitStack

import numpy as np

import concourse.bass as bass
from concourse import mybir

F32 = mybir.dt.float32
F32R = mybir.dt.float32r
ALU = mybir.AluOpType
ACT = mybir.ActivationFunctionType
AX_X = mybir.AxisListType.X

P = 128
S, D, F = 256, 2048, 5504
H = 8
HD = 128
HEADS = 2 * H
M = S // P
KT = D // P
FT = F // P
QKV = 3 * HD
CHUNK, ROPE_HALF, DQK = 64, 8, 64
EPS = 1e-6
NEG = -1e30
LAMBDA_INIT = 0.2

RING = 4
PW = 1024
W0 = 2 * (QKV + H)
W1 = 2 * QKV
IN_PIECES = 8 * HEADS
OUT_PIECES, UP_PIECES, DOWN_PIECES = KT * KT // 8, 2 * FT * KT // 8, FT * KT // 8
OUT0 = IN_PIECES
UP0 = OUT0 + OUT_PIECES
DOWN0 = UP0 + UP_PIECES
ALL_PIECES = DOWN0 + DOWN_PIECES
OCTET = 8
SROW = P + S

C_ID, C_TRI, C_FM, C_DM, C_COS, C_SIN, C_END = np.cumsum([0, P, 2 * P, SROW, SROW, 64, 64]).tolist()
R_FG, R_DG, R_BF, R_LAM, R_END = np.cumsum([0, 2 * HD, 2 * HD, M * H, 4 * DQK]).tolist()
V_G1, V_G2, V_SG, V_CW, V_END = np.cumsum([0, KT, KT, 1, 8 * FT]).tolist()

B_T, B_S, B_O = 4, 5, 7
FORGET_BANKS = (1, 7, 0)

FOX_AT = dict(turn=2, scores=3, probs=5, values=6)
DIFF_AT = dict(turn=3, scores=4)
TRAIL_AT = dict(probs=0, values=1, norm=2)
FORGET_AT = dict(sums=3, rows=4)
OUT_AT = dict(turn=1, scores=2, probs=4, values=5)


def hybrid_layer_kernel(nc, xT_d, w0_d, win_d, wrest_d, const_d, sel_d, row_d, vec_d, out_d):
    with ExitStack() as ctx:
        def sb(name, cols, dt=F32, parts=P, stack=ctx):
            return stack.enter_context(nc.sbuf_tensor(name, [parts, cols], dt))

        def sem(name):
            return ctx.enter_context(nc.semaphore(name))

        ps = ctx.enter_context(nc.psum_tensor("ps", [P, 8 * 512], F32))
        raw = sb("raw", RING * PW)
        w_hi = sb("w_hi", RING * PW, F32R)
        w_lo = sb("w_lo", RING * PW, F32R)
        xT = sb("xT", KT * S)
        xs = sb("xs", KT * 2 * S, F32R)
        vec = sb("vec", V_END)
        r2bc = sb("r2bc", S)
        sqt = sb("sqt", 2 * S)
        accx = sb("accx", PW)
        ones_mean = sb("ones_mean", P)
        lo_t = sb("lo_t", 2 * S)
        s_t = sb("s_t", 2 * S)
        u_t = sb("u_t", 2 * (S + 2))
        y2_t = sb("y2_t", 2 * S)
        y1_t = sb("y1_t", 2 * S)
        silu_t = sb("silu_t", S)
        a_t = sb("a_t", S)
        xu = sb("xu", 2 * S)
        ms2 = y2_t[:, S:2 * S]
        with ExitStack() as att:
            def sa(name, cols, dt=F32, parts=P):
                return sb(name, cols, dt, parts, att)
            mixed = sa("mixed", KT * 2 * S, F32R)
            bias = sa("bias", H * SROW)
            hbias = sa("hbias", SROW)
            const = sa("const", C_END)
            sel = sa("sel", H * P, F32, H)
            row = sa("row", R_END)
            ones_sub = sa("ones_sub", P)
            ones_one = sa("ones_one", P)
            qkv = sa("qkv", 2 * M * QKV)
            xsq = qkv[:, 0:PW]
            sq = sa("sq", M * 2 * HD)
            qn = sa("qn", M * 2 * HD)
            ss, ss2, rs, rsg, nt8 = [sa(n, 8) for n in ("ss", "ss2", "rs", "rsg", "nt8")]
            rms_in, r1g, nt1 = [sa(n, M) for n in ("rms_in", "r1g", "nt1")]
            oms = sa("oms", S)
            org = sa("org", S)
            rope = sa("rope", 4 * 64)
            qkT = sa("qkT", 512)
            s_sb = sa("s_sb", 2 * SROW)
            mx = sa("mx", 4)
            nmx = sa("nmx", 4)
            lsum = sa("lsum", 4)
            rl = sa("rl", 4)
            rll = sa("rll", 2)
            pd = sa("pd", SROW)
            pT = sa("pT", SROW)
            osq = sa("osq", S)
            ors = sa("ors", S)
            on = sa("on", S)
            r1 = sa("r1", M)
            lamt = sa("lamt", 2 * DQK)
            lams = sa("lams", 4)
            z = sa("z", 6 * M * H)
            cT = sa("cT", S, F32, H)
            cq = sa("cq", M * H)
            sg = sa("sg", 1)
        a_s = sb("a_s", FT * 2 * S, F32R)

        x_landed = [sem(f"x_landed{c}") for c in range(4)]
        raw_landed = [sem(f"raw_landed{s}") for s in range(RING)]
        vec_landed, const_landed = sem("vec_landed"), sem("const_landed")
        row_landed, sel_landed = sem("row_landed"), sem("sel_landed")
        ones_set, pad_set = sem("ones_set"), sem("pad_set")
        r1_in, r1_ln, r1_guess, r1_sq, r1_half = [sem("r1_" + n) for n in ("in", "ln", "guess", "sq", "half")]
        rstd_in, rstd_ln, rstd_guess, rstd_sq = [sem("rstd_" + n) for n in ("in", "ln", "guess", "sq")]
        ors_in, ors_ln, ors_guess, ors_sq, ors_half = [sem("ors_" + n) for n in ("in", "ln", "guess", "sq", "half")]
        r2_in, r2_ln, r2_guess, r2_sq, r2_half = [sem("r2_" + n) for n in ("in", "ln", "guess", "sq", "half")]
        xhi_ready, xs_ready = sem("xhi_ready"), sem("xs_ready")
        xsq_step, xsum_ready, rms1_mm, r1_ready = sem("xsq_step"), sem("xsum_ready"), sem("rms1_mm"), sem("r1_ready")
        hi_ready, split_done, piece_used = sem("hi_ready"), sem("split_done"), sem("piece_used")
        evac_done, z_evac = sem("evac_done"), sem("z_evac")
        sumsq_done, rstd_half, rstd_done, normed = sem("sumsq_done"), sem("rstd_half"), sem("rstd_done"), sem("normed")
        rope_prod, rope_done = sem("rope_prod"), sem("rope_done")
        tp_done, qkT_ready, s_done = sem("tp_done"), sem("qkT_ready"), sem("s_done")
        rowmax_done, negmax_done, exp_done = sem("rowmax_done"), sem("negmax_done"), sem("exp_done")
        recip_done, lrecip_done, map2_done, p_ready = sem("recip_done"), sem("lrecip_done"), sem("map2_done"), sem("p_ready")
        pt_done, pT_ready, pv_done = sem("pt_done"), sem("pT_ready"), sem("pv_done")
        osq_done, ors_mm, ors_done, onorm_done = sem("osq_done"), sem("ors_mm"), sem("ors_done"), sem("onorm_done")
        mixhi_done, mixlo_done = sem("mixhi_done"), sem("mixlo_done")
        par_step, lam_sums, lam_exp, lam_ready = sem("par_step"), sem("lam_sums"), sem("lam_exp"), sem("lam_ready")
        z_step, z_exp, nlf_ready, c_mm, c_copied = sem("z_step"), sem("z_exp"), sem("nlf_ready"), sem("c_mm"), sem("c_copied")
        z_abs, z_ln = sem("z_abs"), sem("z_ln")
        cbc_mm, bias_built, head_bias = sem("cbc_mm"), sem("bias_built"), sem("head_bias")
        xu_done, x1_done, x1hi_done, x1sq_done = sem("xu_done"), sem("x1_done"), sem("x1hi_done"), sem("x1sq_done")
        x1sum_done, h2_ready, rms2_mm, r2_ready = sem("x1sum_done"), sem("h2_ready"), sem("rms2_mm"), sem("r2_ready")
        g_lo, g_sum, g_u, g_y2, g_y1, g_y, g_silu = [sem(f"g_{n}") for n in ("lo", "sum", "u", "y2", "y1", "y", "silu")]
        v_lo, v_sum, v_u, v_y2, v_y1, v_y = [sem(f"v_{n}") for n in ("lo", "sum", "u", "y2", "y1", "y")]
        a_done, a_hi, a_lo = sem("a_done"), sem("a_hi"), sem("a_lo")
        ou_done, o_done, stored = sem("ou_done"), sem("o_done"), sem("stored")

        def bank(b, lo=0, n=512):
            return ps[:, b * 512 + lo:b * 512 + lo + n]

        def f32(ap):
            return ap.bitcast(F32)

        def slot(t, s, n=PW, at=0):
            return t[:, s * PW + at:s * PW + at + n]

        def tile(t, i, n=S, width=S, at=0):
            return t[:, bass.ds(i * width + at, n)]

        ident = const[:, C_ID:C_ID + P]
        block = ctx.enter_context(nc.Block())

        @block.sync
        def _(sp):
            for c in range(4):
                w = KT * S // 4
                sp.dma_start(xT[:, c * w:(c + 1) * w], xT_d[:, c * w:(c + 1) * w]).then_inc(x_landed[c], 16)
                sp.dma_start(slot(raw, c, W0), w0_d[c]).then_inc(raw_landed[c], 16)
            for b in range(RING, 8):
                sp.wait_ge(split_done, b - RING + 1)
                sp.dma_start(slot(raw, b % RING, W0), w0_d[b]).then_inc(raw_landed[b % RING], 16)
            with sp.Fori(2, IN_PIECES // RING) as i:
                for b in range(RING):
                    sp.wait_ge(split_done, i * RING + (b - RING + 1))
                    sp.dma_start(slot(raw, b, W1), win_d[bass.ds(i * (RING * P) + (b - 8) * P, P), :]
                                 ).then_inc(raw_landed[b], 16)
            with sp.Fori(IN_PIECES // RING, ALL_PIECES // RING) as i:
                for b in range(RING):
                    sp.wait_ge(split_done, i * RING + (b - RING + 1))
                    sp.dma_start(slot(raw, b), wrest_d[bass.ds(i * (RING * P) + (b - IN_PIECES) * P, P), :]
                                 ).then_inc(raw_landed[b], 16)
            for g in range(ALL_PIECES // RING * RING, ALL_PIECES):
                sp.wait_ge(split_done, g - RING + 1)
                sp.dma_start(slot(raw, g % RING), wrest_d[(g - IN_PIECES) * P:(g - IN_PIECES + 1) * P, :]
                             ).then_inc(raw_landed[g % RING], 16)
            for n in range(KT):
                sp.wait_ge(o_done, n + 1)
                sp.dma_start(out_d[n * P:(n + 1) * P, :], tile(xT, n)).then_inc(stored, 16)
            sp.wait_ge(stored, 16 * KT)

        @block.tensor
        def _(pe):
            def mm3_tokens(p, W, kt, s, k2):
                wh, wl = slot(w_hi, s, W, k2 * W), slot(w_lo, s, W, k2 * W)
                for m in range(M):
                    o = bank(2 * p + m, 0, W)
                    xh = xs[:, kt * 2 * S + m * P:kt * 2 * S + (m + 1) * P]
                    xl = xs[:, kt * 2 * S + S + m * P:kt * 2 * S + S + (m + 1) * P]
                    pe.matmul(o, xh, wh, start=(kt == 0), stop=False, skip_group_check=True)
                    pe.matmul(o, xh, wl, start=False, stop=False, skip_group_check=True)
                    last = pe.matmul(o, xl, wh, start=False, stop=(kt == KT - 1), skip_group_check=True)
                return last

            def mm3_features(b, s, t, act_hilo, act_hi, start, stop):
                pe.matmul(bank(b), slot(w_hi, s, P, t * P), act_hilo, start=start, stop=False, skip_group_check=True)
                return pe.matmul(bank(b, S, S), slot(w_lo, s, P, t * P), act_hi, start=False, stop=stop,
                                 skip_group_check=True)

            def transposes(f, kind):
                pe.wait_ge(normed if kind == "fox" else rope_done, f)
                for i in range(2 * M):
                    qk, m = i // M, i % M
                    last = pe.transpose(bank(B_T, i * P, P), qn[:, m * 2 * HD + qk * HD:m * 2 * HD + (qk + 1) * HD], ident)
                last.then_inc(tp_done, 1)

            def scores(f, kind):
                pe.wait_ge(qkT_ready, f)
                for c in range(1 if kind == "fox" else 2):
                    rows = slice(0, P) if kind == "fox" else slice(c * DQK, (c + 1) * DQK)
                    pe.matmul(bank(B_S + c, 0, P), qkT[rows, 0:P], qkT[rows, S:S + P], start=True, stop=True,
                              skip_group_check=True)
                    last = pe.matmul(bank(B_S + c, P, S), qkT[rows, P:S], qkT[rows, S:2 * S], start=True, stop=True,
                                     skip_group_check=True)
                last.then_inc(s_done, 1)

            def prob_transposes(f, kind):
                pe.wait_ge(p_ready, f)
                src = s_sb if kind == "fox" else pd
                for i in range(3):
                    last = pe.transpose(bank(B_T, i * P, P), src[:, i * P:(i + 1) * P], ident)
                last.then_inc(pt_done, 1)

            def values(f, p, first=False):
                pe.wait_ge(pT_ready, f)
                if not first:
                    pe.wait_ge(mixlo_done, f - 1)
                v = [qkv[:, (p * M + m) * QKV + 2 * HD:(p * M + m + 1) * QKV] for m in range(M)]
                pe.matmul(bank(B_O, 0, S), v[0], pT[:, 0:S], start=True, stop=False, skip_group_check=True)
                pe.matmul(bank(B_O, P, P), v[1], pT[:, S:SROW], start=False, stop=True,
                          skip_group_check=True).then_inc(pv_done, 1)

            def subln_sums(f):
                pe.wait_ge(osq_done, f)
                pe.matmul(bank(B_O, S, S), ones_sub[:], osq[:], start=True, stop=True,
                          skip_group_check=True).then_inc(ors_mm, 1)

            def forget_sums():
                pe.wait_ge(nlf_ready, 1)
                pe.wait_ge(evac_done, 4)
                nlf = [z[:, 5 * M * H + m * H:5 * M * H + (m + 1) * H] for m in range(M)]
                tri, tri_ones = const[:, C_TRI:C_TRI + P], const[:, C_TRI:C_TRI + 2 * P]
                rows = ps[0:H, 0:S]
                pe.matmul(rows, nlf[0], tri_ones, start=True, stop=False, skip_group_check=True)
                pe.matmul(rows[:, P:S], nlf[1], tri, start=False, stop=True, skip_group_check=True)
                pe.matmul(bank(0, S, H), tri, nlf[0], start=True, stop=True, skip_group_check=True)
                pe.matmul(bank(0, S + H, H), tri, nlf[1], start=True, stop=False, skip_group_check=True)
                pe.matmul(bank(0, S + H, H), ones_one[:], nlf[0], start=False, stop=True,
                          skip_group_check=True).then_inc(c_mm, 1)

            def forget_rows(h):
                if h == 0:
                    pe.wait_ge(sel_landed, 16)
                    pe.wait_ge(c_copied, 1)
                if h >= 3:
                    pe.wait_ge(bias_built, h - 2)
                pe.matmul(bank(FORGET_BANKS[h % 3], 0, S), sel[:, h * P:(h + 1) * P], cT[:], start=True, stop=True,
                          skip_group_check=True).then_inc(cbc_mm, 1)

            def attention_steps(f, p, kind, b, at, first=False):
                if b == at["turn"]:
                    transposes(f, kind)
                if b == at["scores"]:
                    scores(f, kind)
                if b == at.get("probs"):
                    prob_transposes(f, kind)
                if b == at.get("values"):
                    values(f, p)
                if first and b == FORGET_AT["sums"]:
                    forget_sums()
                if first and b >= FORGET_AT["rows"]:
                    for h in range(3 * (b - FORGET_AT["rows"]), min(H, 3 * (b - FORGET_AT["rows"]) + 3)):
                        forget_rows(h)

            def trailing_steps(f, p, b, first=False):
                if b == TRAIL_AT["probs"]:
                    prob_transposes(f - 1, "diff")
                if b == TRAIL_AT["values"]:
                    values(f - 1, p, first)
                if b == TRAIL_AT["norm"]:
                    subln_sums(f - 1)

            def frame(f, par, kind, trail=False, first=False, second=False):
                W = QKV + H if kind is None else QKV
                for b in range(8):
                    pe.wait_ge(split_done, f * 8 + (b + 1))
                    if b == 0 and kind is not None and not first:
                        pe.wait_ge(evac_done, f * 4 - 4)
                    if b == 0 and second:
                        pe.wait_ge(bias_built, H)
                    for k2 in range(2):
                        kt = 2 * b + k2
                        if kind is None:
                            pe.wait_ge(xs_ready, kt + 1)
                        last = mm3_tokens(par, W, kt, b % RING, k2)
                    last.then_inc(piece_used, 1)
                    if trail:
                        trailing_steps(f, par, b, first=second)
                    if kind is not None:
                        attention_steps(f, 1 - par, kind, b, FOX_AT if kind == "fox" else DIFF_AT, first)

            frame(0, 0, None)
            pe.wait_ge(xsum_ready, 1)
            pe.wait_ge(ones_set, 1)
            for m in range(M):
                last = pe.matmul(bank(B_O, m, 1), accx[:, m * P:(m + 1) * P], ones_mean[:, 0:1], start=True, stop=True,
                                 skip_group_check=True)
            last.then_inc(rms1_mm, 1)
            pe.wait_ge(const_landed, 16)
            frame(1, 1, "diff", first=True)
            frame(2, 0, "diff", trail=True, second=True)
            frame(3, 1, "diff", trail=True)
            with pe.Fori(2, H // 2) as i:
                frame(i * 2, 0, "diff", trail=True)
                frame(i * 2 + 1, 1, "diff", trail=True)
            frame(H, 0, "diff", trail=True)
            frame(H + 1, 1, "fox", trail=True)
            with pe.Fori(H // 2 + 1, H) as i:
                frame(i * 2, 0, "fox")
                frame(i * 2 + 1, 1, "fox")

            for b in range(8):
                pe.wait_ge(split_done, OUT0 + b + 1)
                for t in range(8):
                    kt, n = 2 * b + t // 4, t % 4
                    if b == 0 and t == 0:
                        pe.wait_ge(mixlo_done, HEADS - 1)
                        pe.wait_ge(evac_done, 4 * (HEADS - 1))
                    if b == 0 and t == 2:
                        pe.wait_ge(evac_done, 4 * HEADS)
                    if kt == KT - 1 and n == 0:
                        pe.wait_ge(mixlo_done, HEADS)
                    mxt = mixed[:, kt * 2 * S:(kt + 1) * 2 * S]
                    last = mm3_features(n, b % RING, t, mxt, mxt[:, 0:S], kt == 0, kt == KT - 1)
                last.then_inc(piece_used, 1)
                attention_steps(HEADS, 1, "fox", b, OUT_AT)

            def out_pair(i, first):
                for b in range(4):
                    pe.wait_ge(split_done, i * 4 + (OUT0 + 8 + b + 1))
                    if b % 2 == 0 and not first:
                        pe.wait_ge(x1_done, i * 2 + (3 + b // 2))
                    for t in range(8):
                        kt = 8 * (b % 2) + t
                        mxt = mixed[:, kt * 2 * S:(kt + 1) * 2 * S]
                        last = mm3_features(4 + b // 2, b, t, mxt, mxt[:, 0:S], kt == 0, kt == KT - 1)
                    last.then_inc(piece_used, 1)

            out_pair(0, True)
            with pe.Fori(1, (KT - 4) // 2) as i:
                out_pair(i, False)

            def up_pair(i, first):
                for b in range(4):
                    pe.wait_ge(split_done, i * 4 + (UP0 + b + 1))
                    if b % 2 == 0 and not first:
                        pe.wait_ge(v_sum if b else g_sum, i)
                    for t in range(8):
                        kt = 8 * (b % 2) + t
                        if first and b < 2:
                            pe.wait_ge(h2_ready, kt + 1)
                        hs = xs[:, kt * 2 * S:(kt + 1) * 2 * S]
                        last = mm3_features(6 + b // 2, b, t, hs, hs[:, 0:S], kt == 0, kt == KT - 1)
                    last.then_inc(piece_used, 1)
                    if first and b == 1:
                        pe.wait_ge(x1sum_done, KT)
                        pe.matmul(bank(0, 0, S), ones_mean[:], accx[:, 0:S], start=True, stop=True,
                                  skip_group_check=True).then_inc(rms2_mm, 1)

            up_pair(0, True)
            with pe.Fori(1, FT) as i:
                up_pair(i, False)

            def down_piece(d, kt, s, edge=None):
                pe.wait_ge(split_done, d + (DOWN0 + 1))
                if edge == "start0":
                    pe.wait_ge(a_lo, FT - 2)
                    pe.wait_ge(r2_ready, 1)
                for n in range(OCTET):
                    if edge == "start0" and n == 6:
                        pe.wait_ge(g_sum, FT)
                        pe.wait_ge(v_sum, FT)
                    if edge == "start1":
                        pe.wait_ge(o_done, n + 1)
                    last = mm3_features(n, s, n, tile(a_s, kt, 2 * S, 2 * S), tile(a_s, kt, S, 2 * S),
                                        edge in ("start0", "start1"), edge == "stop")
                last.then_inc(piece_used, 1)

            for d in range(4):
                down_piece(d, d, d, "start0" if d == 0 else None)
            with pe.Fori(1, 10) as j:
                for b in range(4):
                    down_piece(j * 4 + b, j * 4 + b, b)
            down_piece(40, 40, 0)
            pe.wait_ge(a_lo, FT - 1)
            down_piece(41, 41, 1)
            pe.wait_ge(a_lo, FT)
            down_piece(42, 42, 2, "stop")
            down_piece(43, 0, 3, "start1")
            with pe.Fori(11, 21) as j:
                for b in range(4):
                    down_piece(j * 4 + b, j * 4 + (b - FT), b)
            down_piece(84, 41, 0)
            down_piece(85, 42, 1, "stop")

        @block.scalar
        def _(act):
            def split_hi(G, s, round_, w=PW, free=True):
                act.wait_ge(raw_landed[s], round_ * 16)
                if free:
                    act.wait_ge(piece_used, G - (RING - 1))
                act.activation(slot(w_hi, s, w), slot(raw, s, w), ACT.Copy).then_inc(hi_ready, 1)

            def x_hi(kt):
                if kt % 4 == 0:
                    act.wait_ge(x_landed[kt // 4], 16)
                act.activation(xs[:, kt * 2 * S:kt * 2 * S + S], xT[:, kt * S:(kt + 1) * S], ACT.Copy,
                               scale=vec[:, V_G1 + kt:V_G1 + kt + 1]).then_inc(xhi_ready, 1)

            def evacuate(f, par, n=QKV):
                act.wait_ge(piece_used, f * 8 + 8)
                for m in range(M):
                    act.activation(sq[:, m * 2 * HD:(m + 1) * 2 * HD], bank(2 * par + m, 0, 2 * HD),
                                   ACT.Square, scale=r1[:, m:m + 1]).then_inc(evac_done, 1)
                for m in range(M):
                    act.activation(qkv[:, (par * M + m) * QKV:(par * M + m + 1) * QKV], bank(2 * par + m, 0, QKV),
                                   ACT.Copy, scale=r1[:, m:m + 1]).then_inc(evac_done, 1)

            def guess_rsqrt(y, x, x_ready, ln_done, guess, count):
                act.wait_ge(x_ready, count)
                act.activation(y, x, ACT.Ln).then_inc(ln_done, 1)
                act.wait_ge(ln_done, count)
                act.activation(y, y, ACT.Exp, scale=-0.5).then_inc(guess, 1)

            def copy_qkT(f):
                act.wait_ge(tp_done, f)
                act.activation(qkT[:], bank(B_T), ACT.Copy).then_inc(qkT_ready, 1)

            def exps(f, kind):
                act.wait_ge(negmax_done, f)
                for c in range(1 if kind == "fox" else 2):
                    for qb in range(2):
                        lo, n = c * SROW + qb * P, P * (1 + qb)
                        i = 2 * c + qb
                        last = act.activation(s_sb[:, lo:lo + n], s_sb[:, lo:lo + n], ACT.Exp, bias=nmx[:, i:i + 1],
                                              accum_out=lsum[:, i:i + 1])
                last.then_inc(exp_done, 1)

            def copy_pT(f):
                act.wait_ge(pt_done, f)
                act.activation(pT[:], bank(B_T, 0, SROW), ACT.Copy).then_inc(pT_ready, 1)

            def mix_hi(f, kind):
                act.wait_ge(pv_done if kind == "fox" else onorm_done, f)
                src = bank(B_O, 0, S) if kind == "fox" else on[:]
                act.activation(tile(mixed, f - 1, S, 2 * S), src, ACT.Copy).then_inc(mixhi_done, 1)

            def square_o(f):
                act.wait_ge(pv_done, f)
                act.activation(osq[:], bank(B_O, 0, S), ACT.Square).then_inc(osq_done, 1)

            def attention_steps(f, kind, b, at):
                if b == at["turn"]:
                    copy_qkT(f)
                if b == at["scores"]:
                    exps(f, kind)
                if b == at.get("probs"):
                    copy_pT(f)
                if b == at.get("values"):
                    mix_hi(f, kind)

            def trailing_steps(f, b):
                if b == TRAIL_AT["probs"]:
                    copy_pT(f - 1)
                if b == TRAIL_AT["values"]:
                    square_o(f - 1)
                if b == TRAIL_AT["norm"]:
                    guess_rsqrt(org[:], oms[:], ors_in, ors_ln, ors_guess, f - 1)
                if b == TRAIL_AT["norm"] + 1:
                    mix_hi(f - 1, "diff")

            def head_norm(f, kind):
                n = 4 if kind == "fox" else 8
                guess_rsqrt(rsg[:, 0:n], ss2[:, 0:n], rstd_in, rstd_ln, rstd_guess, f)

            def frame(f, par, kind, next_kind, trail=False, first=False, last=False):
                for b in range(8):
                    if b == 7 and kind is not None:
                        evacuate(f, par)
                        head_norm(f + 1, next_kind)
                    if kind is None and b < 4:
                        x_hi(8 + 2 * b)
                        x_hi(9 + 2 * b)
                    w = PW if last and b >= 4 else W0 if kind is None and b < 4 else W1
                    split_hi(f * 8 + (b + 4), b % RING, f * 2 + (2 + b // 4), w)
                    if kind is not None:
                        attention_steps(f, kind, b, FOX_AT if kind == "fox" else DIFF_AT)
                    if trail:
                        trailing_steps(f, b)
                    if first and b == 1:
                        act.wait_ge(z_abs, 1)
                        act.activation(z[:, 3 * M * H:4 * M * H], z[:, 2 * M * H:3 * M * H], ACT.Exp).then_inc(z_exp, 1)
                        act.wait_ge(z_exp, 1)
                        act.activation(z[:, 4 * M * H:5 * M * H], z[:, 3 * M * H:4 * M * H], ACT.Ln,
                                       bias=1.0).then_inc(z_ln, 1)
                if kind is None:
                    act.wait_ge(lam_sums, 2)
                    act.activation(lams[:, 2:4], lams[:, 0:2], ACT.Exp).then_inc(lam_exp, 1)
                    guess_rsqrt(r1g[:], rms_in[:], r1_in, r1_ln, r1_guess, 1)
                    act.wait_ge(r1_ready, 1)
                    evacuate(f, par)
                    for m in range(M):
                        act.activation(z[:, m * H:(m + 1) * H], bank(m, QKV, H), ACT.Copy,
                                       scale=r1[:, m:m + 1]).then_inc(z_evac, 1)
                    head_norm(f + 1, next_kind)

            act.preload_act_table_set("natural_log_exp_and_others")
            act.wait_ge(vec_landed, 16)
            for b in range(4):
                x_hi(2 * b)
                x_hi(2 * b + 1)
                split_hi(b, b, 1, W0, free=False)
            frame(0, 0, None, "diff")
            frame(1, 1, "diff", "diff", first=True)
            with act.Fori(1, H // 2) as i:
                frame(i * 2, 0, "diff", "diff", trail=True)
                frame(i * 2 + 1, 1, "diff", "diff", trail=True)
            frame(H, 0, "diff", "fox", trail=True)
            frame(H + 1, 1, "fox", "fox", trail=True)
            with act.Fori(H // 2 + 1, H - 1) as i:
                frame(i * 2, 0, "fox", "fox")
                frame(i * 2 + 1, 1, "fox", "fox")
            frame(HEADS - 2, 0, "fox", "fox")
            frame(HEADS - 1, 1, "fox", "fox", last=True)

            def x1_parts(n, par, first=False):
                if not first:
                    act.wait_ge(x1sum_done, n - 1)
                act.wait_ge(x1_done, n + 1)
                act.activation(tile(xs, n, S, 2 * S), tile(xT, n), ACT.Copy,
                               scale=tile(vec, n, 1, 1, V_G2)).then_inc(x1hi_done, 1)
                act.activation(sqt[:, par * S:(par + 1) * S], tile(xT, n), ACT.Square).then_inc(x1sq_done, 1)

            for b in range(8):
                split_hi(OUT0 + b + 4, b % RING, OUT0 // RING + 2 + b // 4)
                attention_steps(HEADS, "fox", b, OUT_AT)
            for n in range(4):
                x1_parts(n, n % 2, n < 2)
            with act.Fori(0, (KT - 4) // 2) as i:
                for b in range(4):
                    split_hi(i * 4 + (OUT0 + 8 + b + 4), b, i + (OUT0 // RING + 4))
                    if b % 2:
                        x1_parts(i * 2 + (4 + b // 2), b // 2)

            def conv_tap2(i, gate):
                u, y2, off = (0, 0, 0) if gate else (S + 2, S, 4)
                act.wait_ge(g_u if gate else v_u, i + 1)
                act.activation(y2_t[:, y2:y2 + S], u_t[:, u + 2:u + 2 + S], ACT.Identity,
                               scale=tile(vec, i, 1, 8, V_CW + off + 2), bias=tile(vec, i, 1, 8, V_CW + off + 3)
                               ).then_inc(g_y2 if gate else v_y2, 1)

            def copy_lo(i, b, gate, first):
                if not first:
                    act.wait_ge(g_sum if gate else v_sum, i)
                lo = 0 if gate else S
                act.activation(lo_t[:, lo:lo + S], bank(6 + (not gate), S, S), ACT.Copy).then_inc(g_lo if gate else v_lo, 1)

            def act_hi(i):
                act.wait_ge(a_done, i + 1)
                act.activation(tile(a_s, i, S, 2 * S), a_t[:], ACT.Copy).then_inc(a_hi, 1)

            def up_frame(i, first):
                for b in range(4):
                    split_hi(i * 4 + (UP0 + b + 4), b, i + (UP0 // RING + 2))
                    if b == 0 and not first:
                        conv_tap2(i - 1, False)
                    if b == 1:
                        if first:
                            guess_rsqrt(sqt[:, 0:S], ms2, r2_in, r2_ln, r2_guess, 1)
                        copy_lo(i, b, True, first)
                        if not first:
                            act_hi(i - 1)
                    if b == 2:
                        conv_tap2(i, True)
                    if b == 3:
                        act.wait_ge(g_y, i + 1)
                        if not first:
                            act.wait_ge(a_done, i)
                        act.activation(silu_t[:], y1_t[:, 0:S], ACT.Silu).then_inc(g_silu, 1)
                        copy_lo(i, b, False, first)

            up_frame(0, True)
            with act.Fori(1, FT) as i:
                up_frame(i, False)
            for s in range(4):
                split_hi(DOWN0 + s + 4, s, DOWN0 // RING + 2)
                if s == 0:
                    conv_tap2(FT - 1, False)
                if s == 1:
                    act_hi(FT - 1)
            with act.Fori(1, 20) as j:
                for b in range(4):
                    split_hi(j * 4 + (DOWN0 + b + 4), b, j + (DOWN0 // RING + 2))
            for s in (80, 81):
                split_hi(DOWN0 + s + 4, s % RING, (DOWN0 + s + 4) // RING + 1)

        @block.vector
        def _(dve):
            def split_lo(G, s, w=PW):
                dve.wait_ge(hi_ready, G + 1)
                dve.tensor_tensor(slot(w_lo, s, w), slot(raw, s, w), f32(slot(w_hi, s, w)),
                                  ALU.subtract).then_inc(split_done, 1)

            def x_lo(kt):
                dve.wait_ge(xhi_ready, kt + 1)
                c = kt * 2 * S
                dve.scalar_tensor_tensor(out=xs[:, c + S:c + 2 * S], in0=xT[:, kt * S:(kt + 1) * S],
                                         scalar=vec[:, V_G1 + kt:V_G1 + kt + 1], in1=f32(xs[:, c:c + S]),
                                         op0=ALU.mult, op1=ALU.subtract).then_inc(xs_ready, 1)

            def newton(out, x, y, t, guess, count, sq_done, half_done, done):
                dve.wait_ge(guess, count)
                dve.tensor_tensor(t, y, y, ALU.mult).then_inc(sq_done, 1)
                dve.wait_ge(sq_done, count)
                dve.scalar_tensor_tensor(out=t, in0=x, scalar=-0.5, in1=t, op0=ALU.mult, op1=ALU.mult).then_inc(half_done, 1)
                dve.wait_ge(half_done, count)
                dve.scalar_tensor_tensor(out=out, in0=t, scalar=1.5, in1=y, op0=ALU.add, op1=ALU.mult).then_inc(done, 1)

            def norm_qk(f, p, kind):
                n = 4 if kind == "fox" else 8
                w = 2 * M * HD // n
                dve.wait_ge(evac_done, f * 4 - 2)
                dve.tensor_reduce(ss[:, 0:n], sq[:].rearrange("p (n w) -> p n w", w=w), AX_X,
                                  ALU.add).then_inc(sumsq_done, 1)
                dve.wait_ge(sumsq_done, f)
                dve.tensor_scalar(ss2[:, 0:n], ss[:, 0:n], float(w * EPS), None, ALU.add).then_inc(rstd_in, 1)
                newton(rs[:, 0:n], ss2[:, 0:n], rsg[:, 0:n], nt8[:, 0:n], rstd_guess, f, rstd_sq, rstd_half, rstd_done)
                dve.wait_ge(rstd_done, f)
                dve.wait_ge(evac_done, f * 4)
                gains = R_FG if kind == "fox" else R_DG
                for m in range(M):
                    for j in range(n // 2):
                        src = qkv[:, (p * M + m) * QKV + j * w:(p * M + m) * QKV + (j + 1) * w]
                        i = m * (n // 2) + j
                        last = dve.scalar_tensor_tensor(
                            out=qn[:, m * 2 * HD + j * w:m * 2 * HD + (j + 1) * w], in0=src, scalar=rs[:, i:i + 1],
                            in1=row[:, gains + j * w:gains + (j + 1) * w], op0=ALU.mult, op1=ALU.mult)
                last.then_inc(normed, 1)

            def row_maxima(f, kind):
                dve.wait_ge(const_landed, 16)
                if kind == "fox":
                    dve.wait_ge(head_bias, f)
                dve.wait_ge(s_done, f)
                n = 2 if kind == "fox" else 4
                for i in range(n):
                    c, lo, w = i // 2, (i % 2) * P, P * (1 + i % 2)
                    add = hbias[:, lo:lo + w] if kind == "fox" else const[:, C_DM + lo:C_DM + lo + w]
                    last = dve.tensor_tensor_reduce(out=s_sb[:, c * SROW + lo:c * SROW + lo + w], in0=bank(B_S + c, lo, w),
                                                    in1=add, scale=1.0, scalar=NEG, op0=ALU.add, op1=ALU.max,
                                                    accum_out=mx[:, i:i + 1])
                last.then_inc(rowmax_done, 1)
                dve.wait_ge(rowmax_done, f)
                dve.tensor_scalar(nmx[:, 0:n], mx[:, 0:n], -1.0, None, ALU.mult).then_inc(negmax_done, 1)

            def normalise(f, kind):
                dve.wait_ge(exp_done, f)
                n = 2 if kind == "fox" else 4
                dve.reciprocal(rl[:, 0:n], lsum[:, 0:n]).then_inc(recip_done, 1)
                dve.wait_ge(recip_done, f)
                if kind == "fox":
                    for qb in range(2):
                        lo, w = qb * P, P * (1 + qb)
                        last = dve.tensor_scalar(s_sb[:, lo:lo + w], s_sb[:, lo:lo + w], rl[:, qb:qb + 1], None, ALU.mult)
                    last.then_inc(p_ready, 1)
                    return
                dve.tensor_scalar(rll[:], rl[:, 2:4], lams[:, 1:2], None, ALU.mult).then_inc(lrecip_done, 1)
                dve.wait_ge(lrecip_done, f)
                for qb in range(2):
                    lo, w = SROW + qb * P, P * (1 + qb)
                    last = dve.tensor_scalar(s_sb[:, lo:lo + w], s_sb[:, lo:lo + w], rll[:, qb:qb + 1], None, ALU.mult)
                last.then_inc(map2_done, 1)
                dve.wait_ge(map2_done, f)
                for qb in range(2):
                    lo, w = qb * P, P * (1 + qb)
                    last = dve.scalar_tensor_tensor(out=pd[:, lo:lo + w], in0=s_sb[:, lo:lo + w], scalar=rl[:, qb:qb + 1],
                                                    in1=s_sb[:, SROW + lo:SROW + lo + w], op0=ALU.mult,
                                                    op1=ALU.subtract)
                last.then_inc(p_ready, 1)

            def mean_square_o(f):
                dve.wait_ge(ors_mm, f)
                dve.tensor_scalar(oms[:], bank(B_O, S, S), EPS, None, ALU.add).then_inc(ors_in, 1)

            def norm_o(f):
                newton(ors[:], oms[:], org[:], osq[:], ors_guess, f, ors_sq, ors_half, ors_done)
                dve.wait_ge(ors_done, f)
                dve.scalar_tensor_tensor(out=on[:], in0=bank(B_O, 0, S), scalar=sg[:], in1=ors[:], op0=ALU.mult,
                                         op1=ALU.mult).then_inc(onorm_done, 1)

            def mix_lo(f, kind):
                dve.wait_ge(mixhi_done, f)
                src = bank(B_O, 0, S) if kind == "fox" else on[:]
                dve.tensor_tensor(tile(mixed, f - 1, S, 2 * S, S), src, f32(tile(mixed, f - 1, S, 2 * S)),
                                  ALU.subtract).then_inc(mixlo_done, 1)

            def forget_bias(h):
                dve.wait_ge(cbc_mm, h + 1)
                for qb in range(2):
                    lo, w = qb * P, P * (1 + qb)
                    last = dve.scalar_tensor_tensor(out=bias[:, h * SROW + lo:h * SROW + lo + w],
                                                    in0=bank(FORGET_BANKS[h % 3], 0, w), scalar=cq[:, qb * H + h:qb * H + h + 1],
                                                    in1=const[:, C_FM + lo:C_FM + lo + w], op0=ALU.subtract,
                                                    op1=ALU.add)
                last.then_inc(bias_built, 1)

            def z_part(i):
                return z[:, i * M * H:(i + 1) * M * H]

            def before_split(f, kind, b, at, trail=False):
                if trail and b == TRAIL_AT["norm"]:
                    mean_square_o(f - 1)
                if trail and b == TRAIL_AT["norm"] + 2:
                    mix_lo(f - 1, "diff")
                if b == at["scores"]:
                    row_maxima(f, kind)
                if b == at["scores"] + (1 if kind == "fox" else 2):
                    normalise(f, kind)

            def after_split(f, kind, b, at, trail=False, first=False):
                if trail and b == TRAIL_AT["norm"]:
                    norm_o(f - 1)
                if b == at.get("values"):
                    mix_lo(f, kind)
                if first and b == 1:
                    dve.wait_ge(z_ln, 1)
                    dve.tensor_tensor(z_part(5), z_part(4), z_part(0), ALU.subtract).then_inc(nlf_ready, 1)
                if first and b == FORGET_AT["sums"]:
                    dve.wait_ge(c_mm, 1)
                    dve.tensor_copy(cT[:], ps[0:H, 0:S])
                    dve.tensor_copy(cq[:], bank(0, S, M * H)).then_inc(c_copied, 1)
                    dve.wait_ge(c_copied, 1)
                if first and b >= FORGET_AT["rows"]:
                    for h in range(3 * (b - FORGET_AT["rows"]), min(H, 3 * (b - FORGET_AT["rows"]) + 3)):
                        forget_bias(h)

            def frame(f, p, kind, next_kind, trail=False, first=False, last=False):
                at = FOX_AT if kind == "fox" else DIFF_AT
                if first:
                    dve.wait_ge(z_evac, M)
                    dve.tensor_tensor(z_part(1), z_part(0), row[:, R_BF:R_BF + M * H], ALU.add).then_inc(z_step, 1)
                    dve.wait_ge(z_step, 1)
                    dve.tensor_scalar(z_part(3), z_part(1), -1.0, None, ALU.mult).then_inc(z_step, 1)
                    dve.wait_ge(z_step, 2)
                    dve.tensor_tensor(z_part(2), z_part(1), z_part(3), ALU.min)
                    dve.tensor_scalar(z_part(0), z_part(1), 0.0, None, ALU.min).then_inc(z_abs, 1)
                for b in range(8):
                    if kind is None and b < 4:
                        x_lo(8 + 2 * b)
                        x_lo(9 + 2 * b)
                    w = PW if last and b >= 4 else W0 if kind is None and b < 4 else W1
                    if kind is not None:
                        before_split(f, kind, b, at, trail)
                        if b == 7:
                            norm_qk(f + 1, 1 - p, next_kind)
                    split_lo(f * 8 + (b + 4), b % RING, w)
                    if kind is not None:
                        after_split(f, kind, b, at, trail, first)

            dve.memset(ones_mean[:], 1.0 / D).then_inc(ones_set, 1)
            dve.memset(ones_sub[:], 1.0 / HD)
            dve.memset(ones_one[:], 1.0)
            dve.memset(u_t[:, 0:2], 0.0)
            dve.memset(u_t[:, S + 2:S + 4], 0.0).then_inc(pad_set, 1)
            for b in range(4):
                if b == 0:
                    dve.wait_ge(vec_landed, 16)
                x_lo(2 * b)
                x_lo(2 * b + 1)
                split_lo(b, b, W0)
            frame(0, 0, None, "diff")
            dve.wait_ge(row_landed, 16)
            dve.tensor_scalar(row[:, R_FG + HD:R_FG + 2 * HD], row[:, R_FG + HD:R_FG + 2 * HD], float(HD) ** 0.5, None,
                              ALU.mult)
            dve.tensor_scalar(row[:, R_DG + HD:R_DG + 2 * HD], row[:, R_DG + HD:R_DG + 2 * HD], float(DQK) ** 0.5, None,
                              ALU.mult)
            dve.tensor_scalar(sg[:], vec[:, V_SG:V_SG + 1], 1.0 - LAMBDA_INIT, None, ALU.mult)
            for c in range(2):
                q, k = R_LAM + 2 * c * DQK, R_LAM + (2 * c + 1) * DQK
                dve.tensor_tensor_reduce(out=lamt[:, c * DQK:(c + 1) * DQK], in0=row[:, q:q + DQK], in1=row[:, k:k + DQK],
                                         scale=1.0, scalar=0.0, op0=ALU.mult, op1=ALU.add,
                                         accum_out=lams[:, c:c + 1]).then_inc(lam_sums, 1)
            dve.wait_ge(rms1_mm, 1)
            dve.tensor_scalar(rms_in[:, 0:M], bank(B_O, 0, M), EPS, None, ALU.add).then_inc(r1_in, 1)
            newton(r1[:], rms_in[:, 0:M], r1g[:], nt1[:], r1_guess, 1, r1_sq, r1_half, r1_ready)
            dve.wait_ge(lam_exp, 1)
            dve.tensor_tensor(lams[:, 0:1], lams[:, 2:3], lams[:, 3:4], ALU.subtract).then_inc(par_step, 1)
            dve.wait_ge(par_step, 1)
            dve.tensor_scalar(lams[:, 1:2], lams[:, 0:1], LAMBDA_INIT, None, ALU.add).then_inc(lam_ready, 1)
            dve.wait_ge(lam_ready, 1)
            dve.wait_ge(const_landed, 16)
            norm_qk(1, 0, "diff")
            frame(1, 0, "diff", "diff", first=True)
            with dve.Fori(1, H // 2) as i:
                frame(i * 2, 1, "diff", "diff", trail=True)
                frame(i * 2 + 1, 0, "diff", "diff", trail=True)
            frame(H, 1, "diff", "fox", trail=True)
            frame(H + 1, 0, "fox", "fox", trail=True)
            with dve.Fori(H // 2 + 1, H - 1) as i:
                frame(i * 2, 1, "fox", "fox")
                frame(i * 2 + 1, 0, "fox", "fox")
            frame(HEADS - 2, 1, "fox", "fox")
            frame(HEADS - 1, 0, "fox", "fox", last=True)

            def x1_tile(n, b, par):
                dve.tensor_tensor(xu[:, par * S:(par + 1) * S], bank(b, S, S), tile(xT, n), ALU.add).then_inc(xu_done, 1)
                dve.wait_ge(xu_done, n + 1)
                dve.tensor_tensor(tile(xT, n), bank(b, 0, S), xu[:, par * S:(par + 1) * S], ALU.add).then_inc(x1_done, 1)

            def x1_lo(n):
                dve.wait_ge(x1hi_done, n + 1)
                dve.scalar_tensor_tensor(out=tile(xs, n, S, 2 * S, S), in0=tile(xT, n), scalar=tile(vec, n, 1, 1, V_G2),
                                         in1=f32(tile(xs, n, S, 2 * S)), op0=ALU.mult,
                                         op1=ALU.subtract).then_inc(h2_ready, 1)

            for b in range(8):
                before_split(HEADS, "fox", b, OUT_AT)
                split_lo(OUT0 + b + 4, b % RING)
                after_split(HEADS, "fox", b, OUT_AT)
            dve.wait_ge(piece_used, OUT0 + 8)
            for n in range(4):
                x1_tile(n, n, n % 2)
                if n:
                    x1_lo(n - 1)
            x1_lo(3)
            with dve.Fori(0, (KT - 4) // 2) as i:
                for b in range(4):
                    split_lo(i * 4 + (OUT0 + 8 + b + 4), b)
                    if b % 2:
                        dve.wait_ge(piece_used, i * 4 + (OUT0 + 8 + b + 1))
                        x1_tile(i * 2 + (4 + b // 2), 4 + b // 2, b // 2)
                        x1_lo(i * 2 + (4 + b // 2))

            def sum_halves(i, gate, first):
                off = 0 if gate else S
                dve.wait_ge(g_lo if gate else v_lo, i + 1)
                if not first:
                    dve.wait_ge(g_u if gate else v_u, i)
                dve.tensor_tensor(s_t[:, off:off + S], bank(6 + (not gate), 0, S), lo_t[:, off:off + S],
                                  ALU.add).then_inc(g_sum if gate else v_sum, 1)

            def conv_taps(i, gate):
                u, off, c = (0, 0, 0) if gate else (S + 2, S, 4)
                y, y1 = (y1_t[:, off:off + S], y2_t[:, off:off + S])
                dve.wait_ge(g_y2 if gate else v_y2, i + 1)
                dve.scalar_tensor_tensor(out=y1, in0=u_t[:, u + 1:u + 1 + S], scalar=tile(vec, i, 1, 8, V_CW + c + 1),
                                         in1=y1, op0=ALU.mult, op1=ALU.add).then_inc(g_y1 if gate else v_y1, 1)
                dve.wait_ge(g_y1 if gate else v_y1, i + 1)
                dve.scalar_tensor_tensor(out=y, in0=u_t[:, u:u + S], scalar=tile(vec, i, 1, 8, V_CW + c),
                                         in1=y1, op0=ALU.mult, op1=ALU.add).then_inc(g_y if gate else v_y, 1)

            def gate_times_value(i):
                dve.wait_ge(v_y, i + 1)
                dve.wait_ge(g_silu, i + 1)
                dve.tensor_tensor(a_t[:], silu_t[:], y1_t[:, S:2 * S], ALU.mult).then_inc(a_done, 1)

            def act_lo(i):
                dve.wait_ge(a_hi, i + 1)
                dve.tensor_tensor(tile(a_s, i, S, 2 * S, S), a_t[:], f32(tile(a_s, i, S, 2 * S)),
                                  ALU.subtract).then_inc(a_lo, 1)

            def up_frame(i, first):
                for b in range(4):
                    split_lo(i * 4 + (UP0 + b + 4), b)
                    if b == 0 and not first:
                        conv_taps(i - 1, False)
                        gate_times_value(i - 1)
                    if b == 1:
                        if first:
                            dve.wait_ge(rms2_mm, 1)
                            dve.tensor_scalar(ms2[:], bank(0, 0, S), EPS, None, ALU.add).then_inc(r2_in, 1)
                            newton(r2bc[:], ms2[:], sqt[:, 0:S], sqt[:, S:2 * S], r2_guess, 1, r2_sq, r2_half, r2_ready)
                        sum_halves(i, True, first)
                        if not first:
                            act_lo(i - 1)
                    if b == 2:
                        conv_taps(i, True)
                    if b == 3:
                        sum_halves(i, False, first)

            up_frame(0, True)
            with dve.Fori(1, FT) as i:
                up_frame(i, False)
            for s in range(4):
                split_lo(DOWN0 + s + 4, s)
                if s == 0:
                    conv_taps(FT - 1, False)
                    gate_times_value(FT - 1)
                if s == 1:
                    act_lo(FT - 1)

            def out_octet(o):
                for n in range(OCTET):
                    t, c = OCTET * o + n, (n % 2) * S
                    dve.tensor_tensor(xu[:, c:c + S], bank(n, S, S), xT[:, t * S:(t + 1) * S], ALU.add).then_inc(ou_done, 1)
                    dve.wait_ge(ou_done, t + 1)
                    dve.tensor_tensor(xT[:, t * S:(t + 1) * S], bank(n, 0, S), xu[:, c:c + S], ALU.add).then_inc(o_done, 1)

            with dve.Fori(1, 10) as j:
                for b in range(4):
                    split_lo(j * 4 + (DOWN0 + b + 4), b)
            for s in (40, 41, 42):
                split_lo(DOWN0 + s + 4, s % RING)
            dve.wait_ge(piece_used, DOWN0 + FT)
            out_octet(0)
            split_lo(DOWN0 + 47, 3)
            with dve.Fori(11, 20) as j:
                for b in range(4):
                    split_lo(j * 4 + (DOWN0 + b + 4), b)
            for s in (80, 81):
                split_lo(DOWN0 + s + 4, s % RING)
            dve.wait_ge(piece_used, DOWN0 + DOWN_PIECES)
            out_octet(1)

        @block.gpsimd
        def _(pool):
            pool.dma_start(vec[:], vec_d).then_inc(vec_landed, 16)
            pool.dma_start(row[:], row_d.partition_broadcast(P)).then_inc(row_landed, 16)
            pool.dma_start(const[:], const_d).then_inc(const_landed, 16)
            pool.dma_start(sel[:], sel_d).then_inc(sel_landed, 16)
            step = 0
            for c in range(4):
                pool.wait_ge(x_landed[c], 16)
                dst = xsq if c else accx[:]
                xc = xT[:, c * PW:(c + 1) * PW]
                if c > 1:
                    pool.wait_ge(xsq_step, step)
                pool.tensor_tensor(dst, xc, xc, ALU.mult).then_inc(xsq_step, 1)
                step += 1
                if c:
                    pool.wait_ge(xsq_step, step)
                    pool.tensor_tensor(accx[:], accx[:], xsq, ALU.add).then_inc(xsq_step, 1)
                    step += 1
            pool.wait_ge(xsq_step, step)
            pool.tensor_tensor(accx[:, 0:512], accx[:, 0:512], accx[:, 512:1024], ALU.add).then_inc(xsq_step, 1)
            pool.wait_ge(xsq_step, step + 1)
            pool.tensor_tensor(accx[:, 0:S], accx[:, 0:S], accx[:, S:2 * S], ALU.add).then_inc(xsum_ready, 1)

            def rotate(f):
                pool.wait_ge(normed, f)
                q4 = qn[:].rearrange("p (n d) -> p n d", d=DQK)
                x1, x2 = q4[:, :, 0:ROPE_HALF], q4[:, :, ROPE_HALF:2 * ROPE_HALF]
                cos = const[:, C_COS:C_COS + 64].rearrange("p (n d) -> p n d", d=ROPE_HALF)
                sin = const[:, C_SIN:C_SIN + 64].rearrange("p (n d) -> p n d", d=ROPE_HALF)
                t = [rope[:, i * 64:(i + 1) * 64].rearrange("p (n d) -> p n d", d=ROPE_HALF) for i in range(4)]
                pool.tensor_tensor(t[0], x1, cos, ALU.mult)
                pool.tensor_tensor(t[1], x2, sin, ALU.mult)
                pool.tensor_tensor(t[2], x2, cos, ALU.mult)
                pool.tensor_tensor(t[3], x1, sin, ALU.mult).then_inc(rope_prod, 1)
                pool.wait_ge(rope_prod, f)
                pool.tensor_tensor(x1, t[0], t[1], ALU.subtract)
                pool.tensor_tensor(x2, t[2], t[3], ALU.add).then_inc(rope_done, 1)

            pool.wait_ge(const_landed, 16)
            with pool.Fori(1, H + 1) as f:
                rotate(f)

            pool.wait_ge(bias_built, 1)
            pool.tensor_copy(hbias[:], bias[:, 0:SROW]).then_inc(head_bias, H + 1)
            with pool.Fori(1, H) as h:
                pool.wait_ge(bias_built, h + 1)
                pool.wait_ge(rowmax_done, h + H)
                pool.tensor_copy(hbias[:], tile(bias, h, SROW, SROW)).then_inc(head_bias, 1)

            for n in range(2):
                pool.wait_ge(x1sq_done, n + 1)
                if n:
                    pool.wait_ge(x1sum_done, n)
                    pool.tensor_tensor(accx[:, 0:S], accx[:, 0:S], sqt[:, S:2 * S], ALU.add).then_inc(x1sum_done, 1)
                else:
                    pool.tensor_copy(accx[:, 0:S], sqt[:, 0:S]).then_inc(x1sum_done, 1)
            with pool.Fori(1, KT // 2) as i:
                for n in range(2):
                    pool.wait_ge(x1sq_done, i * 2 + (n + 1))
                    pool.wait_ge(x1sum_done, i * 2 + n)
                    pool.tensor_tensor(accx[:, 0:S], accx[:, 0:S], sqt[:, n * S:(n + 1) * S], ALU.add).then_inc(x1sum_done, 1)

            pool.wait_ge(pad_set, 1)
            pool.wait_ge(r2_ready, 1)

            def scale_up(i, gate, first):
                off, u = (0, 2) if gate else (S, S + 4)
                pool.wait_ge(g_sum if gate else v_sum, i + 1)
                if not first:
                    pool.wait_ge(g_y if gate else v_y, i)
                pool.tensor_tensor(u_t[:, u:u + S], s_t[:, off:off + S], r2bc[:], ALU.mult).then_inc(g_u if gate else v_u, 1)

            scale_up(0, True, True)
            scale_up(0, False, True)
            with pool.Fori(1, FT) as i:
                scale_up(i, True, False)
                scale_up(i, False, False)


def lay_out(x, norm1_g, w_in, b_forget, fox_q_g, fox_k_g, diff_q_g, diff_k_g, lam_q1, lam_k1, lam_q2, lam_k2,
            diff_subln_g, w_out, norm2_g, w_up, conv_w, conv_b, w_down):
    f = np.ascontiguousarray
    rows = lambda a: a[0].reshape(KT, P, -1)
    w = np.asarray(w_in)[0]
    fw = H * HD
    cut = [w[:, i * fw:(i + 1) * fw] for i in range(3)] + [w[:, 3 * fw + H + i * fw:3 * fw + H + (i + 1) * fw] for i in range(3)]
    flog = w[:, 3 * fw:3 * fw + H]

    def head(j):
        q, k, v = cut[3:6] if j < H else cut[0:3]
        c = slice((j % H) * HD, (j % H + 1) * HD)
        cols = [q[:, c], k[:, c], v[:, c]] + ([flog] if j == 0 else [])
        a = np.concatenate(cols, axis=1)
        return a.reshape(8, 2, P, -1).transpose(0, 2, 1, 3).reshape(8, P, -1)

    win = np.concatenate([head(j) for j in range(1, HEADS)]).reshape(-1, W1)
    wo = np.asarray(w_out)[0].reshape(KT, P, KT, P)
    wo = np.concatenate([wo[H:], wo[:H]])
    out0 = wo[:, :, 0:4].reshape(8, 2, P, 4, P).transpose(0, 2, 1, 3, 4).reshape(8 * P, PW)
    out1 = wo[:, :, 4:].reshape(2, 8, P, KT - 4, P).transpose(3, 0, 2, 1, 4).reshape(-1, PW)
    wu = np.asarray(w_up)[0].reshape(2, 8, P, 2, FT, P)
    up = wu.transpose(4, 3, 0, 2, 1, 5).reshape(-1, PW)
    wd = np.asarray(w_down)[0].reshape(FT, P, 2, PW)
    down = wd.transpose(2, 0, 1, 3).reshape(-1, PW)

    i = np.arange(P)
    tri = (i[:, None] <= i[None, :]).astype(np.float32)
    causal = np.where(i[None, :] <= i[:, None], 0.0, NEG).astype(np.float32)
    chunk = np.where(i[None, :] // CHUNK <= i[:, None] // CHUNK, 0.0, NEG).astype(np.float32)
    zero = np.zeros((P, P), np.float32)
    inv = (np.float32(500000.0) ** (-np.arange(0, 16, 2, dtype=np.float32) / np.float32(16))).astype(np.float32)
    ang = np.arange(S, dtype=np.float32)[:, None] * inv[None, :]
    trig = lambda fn: np.tile(fn(ang).astype(np.float32).reshape(M, P, 1, ROPE_HALF), (1, 1, 4, 1)).transpose(1, 0, 2, 3).reshape(P, -1)
    const = np.concatenate([np.eye(P, dtype=np.float32), tri, np.ones((P, P), np.float32), causal, zero, causal,
                            chunk, zero, chunk, trig(np.cos), trig(np.sin)], axis=1)
    sel = np.repeat(np.eye(H, dtype=np.float32), P, axis=1)

    dq, dk = diff_q_g[0], diff_k_g[0]
    row = np.concatenate([fox_q_g[0], fox_k_g[0], dq, dq, dk, dk, b_forget[0], b_forget[0],
                          lam_q1[0], lam_k1[0], lam_q2[0], lam_k2[0]])[None]
    cw = np.concatenate([np.asarray(conv_w)[0], np.asarray(conv_b)], axis=0)
    cw = cw.reshape(4, 2, FT, P).transpose(3, 2, 1, 0).reshape(P, -1)
    vec = np.concatenate([norm1_g[0].reshape(KT, P).T, norm2_g[0].reshape(KT, P).T, diff_subln_g[0][:, None], cw], axis=1)
    xT = np.asarray(x)[0].T.reshape(KT, P, S).transpose(1, 0, 2).reshape(P, -1)
    return dict(xT=f(xT), w0=f(head(0)), win=f(win), wrest=f(np.concatenate([out0, out1, up, down])), const=f(const),
                sel=f(sel), row=f(row), vec=f(vec))


def kernel(**inputs):
    import concourse.bacc as bacc
    from concourse.bass_utils import run_bass_kernel_spmd

    arrays = lay_out(**{k: np.asarray(v) for k, v in inputs.items()})
    nc = bacc.Bacc("TRN2", target_bir_lowering=False, num_devices=1)
    args = [nc.dram_tensor("in_" + n, a.shape, F32, kind="ExternalInput").ap() for n, a in arrays.items()]
    out = nc.dram_tensor("out", (D, S), F32, kind="ExternalOutput").ap()
    hybrid_layer_kernel(nc, *args, out)
    got = run_bass_kernel_spmd(nc, [{"in_" + n: a for n, a in arrays.items()}], core_ids=[0]).results[0]["out"]
    return np.ascontiguousarray(got.T).reshape(1, S, D)
```

```python
from contextlib import ExitStack

import numpy as np

import concourse.bass as bass
from concourse import mybir

F32 = mybir.dt.float32
F32R = mybir.dt.float32r
ALU = mybir.AluOpType
ACT = mybir.ActivationFunctionType
AX_X = mybir.AxisListType.X

P = 128
S, D, F = 256, 2048, 5504
H = 8
HD = 128
HEADS = 2 * H
M = S // P
KT = D // P
FT = F // P
QKV = 3 * HD
CHUNK, ROPE_HALF, DQK = 64, 8, 64
EPS = 1e-6
NEG = -1e30
LAMBDA_INIT = 0.2

RING = 4
PW = 1024
W0 = 2 * (QKV + H)
W1 = 2 * QKV
WARM_UP = 14
ACT_SQUARES = (2, 5)
SUM_ORDER = (0, 1, 3, 2, 4, 6, 5, 7)
XW = 2 * S
IN_PIECES = 8 * HEADS
OUT_PIECES, UP_PIECES, DOWN_PIECES = KT * KT // 8, 2 * FT * KT // 8, FT * KT // 8
OUT0 = IN_PIECES
UP0 = OUT0 + OUT_PIECES
DOWN0 = UP0 + UP_PIECES
ALL_PIECES = DOWN0 + DOWN_PIECES
OCTET = 8
SROW = P + S

C_ID, C_TRI, C_FM, C_DM, C_COS, C_SIN, C_END = np.cumsum([0, P, 2 * P, SROW, SROW, 64, 64]).tolist()
R_FG, R_DG, R_BF, R_LAM, R_END = np.cumsum([0, 2 * HD, 2 * HD, M * H, 4 * DQK]).tolist()
V_G1, V_G2, V_SG, V_CW, V_END = np.cumsum([0, KT, KT, 1, 8 * FT]).tolist()

B_T, B_S, B_O = 4, 5, 7
FORGET_BANKS = (1, 0, 7, 1, 0, 7, 6, 7)

FOX_AT = dict(turn=2, scores=3, probs=5, values=6)
FOX1_AT = dict(turn=2, scores=3, probs=6, values=7)
DIFF1_AT = dict(turn=4, scores=5)
DIFF_AT = dict(turn=3, scores=4)
TRAIL_AT = dict(probs=1, values=2, norm=3)
FORGET_AT = dict(sums=3, rows=(4, 4, 4, 5, 5, 5, 6, 7))
OUT_AT = dict(turn=1, scores=2, probs=4, values=5)


def hybrid_layer_kernel(nc, xT_d, w0_d, win_d, wrest_d, const_d, sel_d, row_d, vec_d, out_d):
    with ExitStack() as ctx:
        def sb(name, cols, dt=F32, parts=P, stack=ctx):
            return stack.enter_context(nc.sbuf_tensor(name, [parts, cols], dt))

        def sem(name):
            return ctx.enter_context(nc.semaphore(name))

        ps = ctx.enter_context(nc.psum_tensor("ps", [P, 8 * 512], F32))
        raw = sb("raw", RING * PW)
        w_hi = sb("w_hi", RING * PW, F32R)
        w_lo = sb("w_lo", RING * PW, F32R)
        xT = sb("xT", KT * S)
        xs = sb("xs", KT * 2 * S, F32R)
        vec = sb("vec", V_END)
        r2bc = sb("r2bc", S)
        sqt = sb("sqt", 2 * S)
        accx = sb("accx", XW)
        ones_mean = sb("ones_mean", P)
        lo_t = sb("lo_t", 2 * S)
        s_t = sb("s_t", 2 * S)
        u_t = sb("u_t", 2 * (S + 2))
        y2_t = sb("y2_t", 2 * S)
        y1_t = sb("y1_t", 2 * S)
        silu_t = sb("silu_t", S)
        a_t = sb("a_t", S)
        xu = sb("xu", 2 * S)
        ms2 = y2_t[:, S:2 * S]
        with ExitStack() as att:
            def sa(name, cols, dt=F32, parts=P):
                return sb(name, cols, dt, parts, att)
            mixed = sa("mixed", KT * 2 * S, F32R)
            bias = sa("bias", H * SROW)
            hbias = sa("hbias", SROW)
            const = sa("const", C_END)
            sel = sa("sel", H * P, F32, H)
            row = sa("row", R_END)
            ones_sub = sa("ones_sub", P)
            ones_one = sa("ones_one", P)
            qkv = sa("qkv", 2 * M * QKV)
            xsq = qkv[:, 0:XW]
            sq = sa("sq", M * 2 * HD)
            qn = sa("qn", M * 2 * HD)
            ss, ss2, rs, rsg, nt8 = [sa(n, 8) for n in ("ss", "ss2", "rs", "rsg", "nt8")]
            rms_in, r1g, nt1 = [sa(n, M) for n in ("rms_in", "r1g", "nt1")]
            oms = sa("oms", S)
            org = sa("org", S)
            rope = sa("rope", 4 * 64)
            qkT = sa("qkT", 512)
            s_sb = sa("s_sb", 2 * SROW)
            mx = sa("mx", 4)
            nmx = sa("nmx", 4)
            lsum = sa("lsum", 4)
            rl = sa("rl", 4)
            rll = sa("rll", 2)
            pd = sa("pd", SROW)
            pT = sa("pT", SROW)
            osq = sa("osq", S)
            ors = sa("ors", S)
            on = sa("on", S)
            r1 = sa("r1", M)
            lamt = sa("lamt", 2 * DQK)
            lams = sa("lams", 4)
            z = sa("z", 6 * M * H)
            cT = sa("cT", S, F32, H)
            cq = sa("cq", M * H)
            sg = sa("sg", 1)
        a_s = sb("a_s", FT * 2 * S, F32R)

        x_landed = [sem(f"x_landed{c}") for c in range(8)]
        raw_landed = [sem(f"raw_landed{s}") for s in range(RING)]
        vec_landed, conv_landed, const_landed = sem("vec_landed"), sem("conv_landed"), sem("const_landed")
        row_landed, sel_landed = sem("row_landed"), sem("sel_landed")
        ones_set, pad_set = sem("ones_set"), sem("pad_set")
        r1_in, r1_ln, r1_guess, r1_sq, r1_half = [sem("r1_" + n) for n in ("in", "ln", "guess", "sq", "half")]
        rstd_in, rstd_ln, rstd_guess, rstd_sq = [sem("rstd_" + n) for n in ("in", "ln", "guess", "sq")]
        ors_in, ors_ln, ors_guess, ors_sq, ors_half = [sem("ors_" + n) for n in ("in", "ln", "guess", "sq", "half")]
        r2_in, r2_ln, r2_guess, r2_sq, r2_half = [sem("r2_" + n) for n in ("in", "ln", "guess", "sq", "half")]
        xhi_ready, xs_ready = sem("xhi_ready"), sem("xs_ready")
        xsq_step, xsq_act, rms1_mm, r1_ready = sem("xsq_step"), sem("xsq_act"), sem("rms1_mm"), sem("r1_ready")
        hi_ready, split_done, piece_used = sem("hi_ready"), sem("split_done"), sem("piece_used")
        evac_done, z_evac = sem("evac_done"), sem("z_evac")
        sumsq_done, rstd_half, rstd_done, normed = sem("sumsq_done"), sem("rstd_half"), sem("rstd_done"), sem("normed")
        gains_ready, gained = sem("gains_ready"), sem("gained")
        rope_prod, rope_done = sem("rope_prod"), sem("rope_done")
        tp_done, qkT_ready, s_done = sem("tp_done"), sem("qkT_ready"), sem("s_done")
        rowmax_done, negmax_done, exp_done = sem("rowmax_done"), sem("negmax_done"), sem("exp_done")
        recip_done, lrecip_done, map2_done, p_ready = sem("recip_done"), sem("lrecip_done"), sem("map2_done"), sem("p_ready")
        pt_done, pT_ready, pv_done = sem("pt_done"), sem("pT_ready"), sem("pv_done")
        osq_done, ors_mm, ors_done, onorm_done = sem("osq_done"), sem("ors_mm"), sem("ors_done"), sem("onorm_done")
        mixhi_done, mixlo_done = sem("mixhi_done"), sem("mixlo_done")
        par_step, lam_sums, lam_exp, lam_ready = sem("par_step"), sem("lam_sums"), sem("lam_exp"), sem("lam_ready")
        z_step, z_exp, nlf_ready, c_mm, c_copied = sem("z_step"), sem("z_exp"), sem("nlf_ready"), sem("c_mm"), sem("c_copied")
        z_abs, z_ln = sem("z_abs"), sem("z_ln")
        cbc_mm, bias_built, head_bias = sem("cbc_mm"), sem("bias_built"), sem("head_bias")
        xu_done, x1_done, x1hi_done, x1sq_done = sem("xu_done"), sem("x1_done"), sem("x1hi_done"), sem("x1sq_done")
        x1sum_done, h2_ready, rms2_mm, r2_ready = sem("x1sum_done"), sem("h2_ready"), sem("rms2_mm"), sem("r2_ready")
        g_lo, g_sum, g_u, g_y2, g_y1, g_y, g_silu = [sem(f"g_{n}") for n in ("lo", "sum", "u", "y2", "y1", "y", "silu")]
        v_lo, v_sum, v_u, v_y2, v_y1, v_y = [sem(f"v_{n}") for n in ("lo", "sum", "u", "y2", "y1", "y")]
        a_done, a_hi, a_lo = sem("a_done"), sem("a_hi"), sem("a_lo")
        tile_summed = sem("tile_summed")
        ou_done, o_done, stored = sem("ou_done"), sem("o_done"), sem("stored")

        def bank(b, lo=0, n=512):
            return ps[:, b * 512 + lo:b * 512 + lo + n]

        def f32(ap):
            return ap.bitcast(F32)

        def slot(t, s, n=PW, at=0):
            return t[:, s * PW + at:s * PW + at + n]

        def tile(t, i, n=S, width=S, at=0):
            return t[:, bass.ds(i * width + at, n)]

        ident = const[:, C_ID:C_ID + P]
        block = ctx.enter_context(nc.Block())

        @block.sync
        def _(sp):
            sp.dma_start(vec[:, 0:V_CW], vec_d[:, 0:V_CW]).then_inc(vec_landed, 16)
            for c in range(8):
                sp.dma_start(xT[:, c * XW:(c + 1) * XW], xT_d[:, c * XW:(c + 1) * XW]).then_inc(x_landed[c], 16)
                if c >= RING:
                    sp.wait_ge(split_done, c - RING + 1)
                sp.dma_start(slot(raw, c % RING, W0), w0_d[c]).then_inc(raw_landed[c % RING], 16)
            sp.dma_start(row[:], row_d.partition_broadcast(P)).then_inc(row_landed, 16)

            def in_pieces(i):
                for b in range(RING):
                    sp.wait_ge(split_done, i * RING + (b - RING + 1))
                    sp.dma_start(slot(raw, b, W1), win_d[bass.ds(i * (RING * P) + (b - 8) * P, P), :]
                                 ).then_inc(raw_landed[b], 16)

            in_pieces(2)
            sp.dma_start(const[:], const_d).then_inc(const_landed, 16)
            sp.dma_start(sel[:], sel_d).then_inc(sel_landed, 16)
            with sp.Fori(3, IN_PIECES // RING) as i:
                in_pieces(i)
            sp.dma_start(vec[:, V_CW:V_END], vec_d[:, V_CW:V_END]).then_inc(conv_landed, 16)
            with sp.Fori(IN_PIECES // RING, ALL_PIECES // RING) as i:
                for b in range(RING):
                    sp.wait_ge(split_done, i * RING + (b - RING + 1))
                    sp.dma_start(slot(raw, b), wrest_d[bass.ds(i * (RING * P) + (b - IN_PIECES) * P, P), :]
                                 ).then_inc(raw_landed[b], 16)
            for g in range(ALL_PIECES // RING * RING, ALL_PIECES):
                sp.wait_ge(split_done, g - RING + 1)
                sp.dma_start(slot(raw, g % RING), wrest_d[(g - IN_PIECES) * P:(g - IN_PIECES + 1) * P, :]
                             ).then_inc(raw_landed[g % RING], 16)
            for n in range(KT):
                sp.wait_ge(o_done, n + 1)
                sp.dma_start(out_d[n * P:(n + 1) * P, :], tile(xT, n)).then_inc(stored, 16)
            sp.wait_ge(stored, 16 * KT)

        @block.tensor
        def _(pe):
            def mm3_tokens(p, W, kt, s, k2):
                wh, wl = slot(w_hi, s, W, k2 * W), slot(w_lo, s, W, k2 * W)
                for m in range(M):
                    o = bank(2 * p + m, 0, W)
                    xh = xs[:, kt * 2 * S + m * P:kt * 2 * S + (m + 1) * P]
                    xl = xs[:, kt * 2 * S + S + m * P:kt * 2 * S + S + (m + 1) * P]
                    pe.matmul(o, xh, wh, start=(kt == 0), stop=False, skip_group_check=True)
                    pe.matmul(o, xh, wl, start=False, stop=False, skip_group_check=True)
                    last = pe.matmul(o, xl, wh, start=False, stop=(kt == KT - 1), skip_group_check=True)
                return last

            def mm3_features(b, s, t, act_hilo, act_hi, start, stop):
                pe.matmul(bank(b), slot(w_hi, s, P, t * P), act_hilo, start=start, stop=False, skip_group_check=True)
                return pe.matmul(bank(b, S, S), slot(w_lo, s, P, t * P), act_hi, start=False, stop=stop,
                                 skip_group_check=True)

            def transposes(f, kind):
                pe.wait_ge(normed if kind == "fox" else rope_done, f)
                for i in range(2 * M):
                    qk, m = i // M, i % M
                    last = pe.transpose(bank(B_T, i * P, P), qn[:, m * 2 * HD + qk * HD:m * 2 * HD + (qk + 1) * HD], ident)
                last.then_inc(tp_done, 1)

            def scores(f, kind):
                pe.wait_ge(qkT_ready, f)
                for c in range(1 if kind == "fox" else 2):
                    rows = slice(0, P) if kind == "fox" else slice(c * DQK, (c + 1) * DQK)
                    pe.matmul(bank(B_S + c, 0, P), qkT[rows, 0:P], qkT[rows, S:S + P], start=True, stop=True,
                              skip_group_check=True)
                    last = pe.matmul(bank(B_S + c, P, S), qkT[rows, P:S], qkT[rows, S:2 * S], start=True, stop=True,
                                     skip_group_check=True)
                last.then_inc(s_done, 1)

            def prob_transposes(f, kind):
                pe.wait_ge(p_ready, f)
                src = s_sb if kind == "fox" else pd
                for i in range(3):
                    last = pe.transpose(bank(B_T, i * P, P), src[:, i * P:(i + 1) * P], ident)
                last.then_inc(pt_done, 1)

            def values(f, p, first=False):
                pe.wait_ge(pT_ready, f)
                if first:
                    pe.wait_ge(bias_built, H)
                else:
                    pe.wait_ge(mixlo_done, f - 1)
                v = [qkv[:, (p * M + m) * QKV + 2 * HD:(p * M + m + 1) * QKV] for m in range(M)]
                pe.matmul(bank(B_O, 0, S), v[0], pT[:, 0:S], start=True, stop=False, skip_group_check=True)
                pe.matmul(bank(B_O, P, P), v[1], pT[:, S:SROW], start=False, stop=True,
                          skip_group_check=True).then_inc(pv_done, 1)

            def subln_sums(f):
                pe.wait_ge(osq_done, f)
                pe.matmul(bank(B_O, S, S), ones_sub[:], osq[:], start=True, stop=True,
                          skip_group_check=True).then_inc(ors_mm, 1)

            def forget_sums():
                pe.wait_ge(const_landed, 16)
                pe.wait_ge(nlf_ready, 1)
                pe.wait_ge(evac_done, 4)
                nlf = [z[:, 5 * M * H + m * H:5 * M * H + (m + 1) * H] for m in range(M)]
                tri, tri_ones = const[:, C_TRI:C_TRI + P], const[:, C_TRI:C_TRI + 2 * P]
                rows = ps[0:H, 0:S]
                pe.matmul(rows, nlf[0], tri_ones, start=True, stop=False, skip_group_check=True)
                pe.matmul(rows[:, P:S], nlf[1], tri, start=False, stop=True, skip_group_check=True)
                pe.matmul(bank(0, S, H), tri, nlf[0], start=True, stop=True, skip_group_check=True)
                pe.matmul(bank(0, S + H, H), tri, nlf[1], start=True, stop=False, skip_group_check=True)
                pe.matmul(bank(0, S + H, H), ones_one[:], nlf[0], start=False, stop=True,
                          skip_group_check=True).then_inc(c_mm, 1)

            def forget_rows(h):
                if h == 0:
                    pe.wait_ge(sel_landed, 16)
                    pe.wait_ge(c_copied, 1)
                if h == 6:
                    pe.wait_ge(rowmax_done, 1)
                if h in (3, 4, 5, 7):
                    pe.wait_ge(bias_built, 6 if h == 7 else h - 2)
                pe.matmul(bank(FORGET_BANKS[h], 0, S), sel[:, h * P:(h + 1) * P], cT[:], start=True, stop=True,
                          skip_group_check=True).then_inc(cbc_mm, 1)

            def attention_steps(f, p, kind, b, at, first=False):
                if b == at["turn"]:
                    if first:
                        pe.wait_ge(const_landed, 16)
                    transposes(f, kind)
                if b == at["scores"]:
                    scores(f, kind)
                if b == at.get("probs"):
                    prob_transposes(f, kind)
                if b == at.get("values"):
                    values(f, p)
                if first and b == FORGET_AT["sums"]:
                    forget_sums()
                for h in range(H):
                    if first and b == FORGET_AT["rows"][h]:
                        forget_rows(h)

            def trailing_steps(f, p, b, first=False):
                if b == TRAIL_AT["probs"]:
                    prob_transposes(f - 1, "diff")
                if b == TRAIL_AT["values"]:
                    values(f - 1, p, first)
                if b == TRAIL_AT["norm"]:
                    subln_sums(f - 1)

            def frame(f, par, kind, at=None, trail=False, first=False, second=False):
                W = QKV + H if kind is None else QKV
                for b in range(8):
                    pe.wait_ge(split_done, f * 8 + (b + 1))
                    if b == 0 and kind is not None and not first:
                        pe.wait_ge(evac_done, f * 4 - 4)
                    if b == 0 and second:
                        pe.wait_ge(bias_built, 5)
                    for k2 in range(2):
                        kt = 2 * b + k2
                        if kind is None:
                            pe.wait_ge(xs_ready, kt + 1)
                        last = mm3_tokens(par, W, kt, b % RING, k2)
                    last.then_inc(piece_used, 1)
                    if trail:
                        trailing_steps(f, par, b, first=second)
                    if kind is not None:
                        attention_steps(f, 1 - par, kind, b, at, first)

            pe.wait_ge(ones_set, 1)
            for _ in range(WARM_UP):
                pe.matmul(bank(B_S + 1, 0, P), ones_mean[:], ones_mean[:], start=True, stop=True, skip_group_check=True)
            frame(0, 0, None)
            pe.wait_ge(xsq_step, 15)
            for m in range(M):
                for k in range(2):
                    last = pe.matmul(bank(B_O, m, 1), accx[:, k * S + m * P:k * S + (m + 1) * P], ones_mean[:, 0:1],
                                     start=(k == 0), stop=(k == 1), skip_group_check=True)
            last.then_inc(rms1_mm, 1)
            frame(1, 1, "diff", DIFF1_AT, first=True)
            frame(2, 0, "diff", DIFF_AT, trail=True, second=True)
            frame(3, 1, "diff", DIFF_AT, trail=True)
            with pe.Fori(2, H // 2) as i:
                frame(i * 2, 0, "diff", DIFF_AT, trail=True)
                frame(i * 2 + 1, 1, "diff", DIFF_AT, trail=True)
            frame(H, 0, "diff", DIFF_AT, trail=True)
            frame(H + 1, 1, "fox", FOX1_AT, trail=True)
            with pe.Fori(H // 2 + 1, H) as i:
                frame(i * 2, 0, "fox", FOX_AT)
                frame(i * 2 + 1, 1, "fox", FOX_AT)

            for b in range(8):
                pe.wait_ge(split_done, OUT0 + b + 1)
                for t in (0, 1, 4, 5, 2, 6, 3, 7) if b == 0 else range(8):
                    kt, n = 2 * b + t // 4, t % 4
                    if b == 0 and t == 0:
                        pe.wait_ge(evac_done, 4 * (HEADS - 1))
                    if b == 0 and t in (2, 3):
                        pe.wait_ge(evac_done, 4 * HEADS - 3 + t)
                    if kt >= KT - 2 and n == 0:
                        pe.wait_ge(mixlo_done, kt + 1)
                    mxt = mixed[:, kt * 2 * S:(kt + 1) * 2 * S]
                    last = mm3_features(n, b % RING, t, mxt, mxt[:, 0:S], kt == 0, kt == KT - 1)
                last.then_inc(piece_used, 1)
                attention_steps(HEADS, 1, "fox", b, OUT_AT)

            def out_pair(i, first):
                for b in range(4):
                    pe.wait_ge(split_done, i * 4 + (OUT0 + 8 + b + 1))
                    if b % 2 == 0 and not first:
                        pe.wait_ge(x1_done, i * 2 + (3 + b // 2))
                    for t in range(8):
                        kt = 8 * (b % 2) + t
                        mxt = mixed[:, kt * 2 * S:(kt + 1) * 2 * S]
                        last = mm3_features(4 + b // 2, b, t, mxt, mxt[:, 0:S], kt == 0, kt == KT - 1)
                    last.then_inc(piece_used, 1)

            out_pair(0, True)
            with pe.Fori(1, (KT - 4) // 2) as i:
                out_pair(i, False)

            def up_pair(i, first):
                for b in range(4):
                    pe.wait_ge(split_done, i * 4 + (UP0 + b + 1))
                    if b % 2 == 0 and not first:
                        pe.wait_ge(v_sum if b else g_sum, i)
                    for t in range(8):
                        kt = 8 * (b % 2) + t
                        if first and b < 2:
                            pe.wait_ge(h2_ready, kt + 1)
                        hs = xs[:, kt * 2 * S:(kt + 1) * 2 * S]
                        last = mm3_features(6 + b // 2, b, t, hs, hs[:, 0:S], kt == 0, kt == KT - 1)
                    last.then_inc(piece_used, 1)
                    if first and b == 1:
                        pe.wait_ge(x1sum_done, KT)
                        pe.matmul(bank(0, 0, S), ones_mean[:], accx[:, 0:S], start=True, stop=True,
                                  skip_group_check=True).then_inc(rms2_mm, 1)

            up_pair(0, True)
            with pe.Fori(1, FT) as i:
                up_pair(i, False)

            def down_piece(d, kt, s, edge=None):
                pe.wait_ge(split_done, d + (DOWN0 + 1))
                if edge == "start0":
                    pe.wait_ge(a_lo, FT - 2)
                    pe.wait_ge(r2_ready, 1)
                for n in range(OCTET):
                    if edge == "start0" and n == 6:
                        pe.wait_ge(g_sum, FT)
                        pe.wait_ge(v_sum, FT)
                    if edge == "start1":
                        pe.wait_ge(o_done, n + 1)
                    last = mm3_features(n, s, n, tile(a_s, kt, 2 * S, 2 * S), tile(a_s, kt, S, 2 * S),
                                        edge in ("start0", "start1"), False)
                last.then_inc(piece_used, 1)

            def last_two(d, s):
                pe.wait_ge(split_done, DOWN0 + d + 2)
                for n in range(OCTET):
                    for k in range(2):
                        kt = FT - 2 + k
                        a = a_s[:, kt * 2 * S:(kt + 1) * 2 * S]
                        last = mm3_features(n, s + k, n, a, a[:, 0:S], False, k == 1)
                    if n < OCTET - 1:
                        last.then_inc(tile_summed, 1)
                last.then_inc(piece_used, 2)

            for d in range(4):
                down_piece(d, d, d, "start0" if d == 0 else None)
            with pe.Fori(1, 10) as j:
                for b in range(4):
                    down_piece(j * 4 + b, j * 4 + b, b)
            down_piece(40, 40, 0)
            pe.wait_ge(a_lo, FT)
            last_two(41, 1)
            down_piece(43, 0, 3, "start1")
            with pe.Fori(11, 21) as j:
                for b in range(4):
                    down_piece(j * 4 + b, j * 4 + (b - FT), b)
            last_two(84, 0)

        @block.scalar
        def _(act):
            def split_hi(G, s, round_, w=PW, free=True):
                act.wait_ge(raw_landed[s], round_ * 16)
                if free:
                    act.wait_ge(piece_used, G - (RING - 1))
                act.activation(slot(w_hi, s, w), slot(raw, s, w), ACT.Copy).then_inc(hi_ready, 1)

            def x_hi(kt):
                if kt % 2 == 0:
                    act.wait_ge(x_landed[kt // 2], 16)
                act.activation(xs[:, kt * 2 * S:kt * 2 * S + S], xT[:, kt * S:(kt + 1) * S], ACT.Copy,
                               scale=vec[:, V_G1 + kt:V_G1 + kt + 1]).then_inc(xhi_ready, 1)

            def x_squares(c):
                if c != ACT_SQUARES[0]:
                    act.wait_ge(xsq_step, 2 * SUM_ORDER.index(ACT_SQUARES[0]) + 1)
                act.activation(sq[:], xT[:, c * XW:(c + 1) * XW], ACT.Square).then_inc(xsq_act, 1)

            def evacuate(f, par, n=QKV):
                act.wait_ge(piece_used, f * 8 + 8)
                for m in range(M):
                    act.activation(sq[:, m * 2 * HD:(m + 1) * 2 * HD], bank(2 * par + m, 0, 2 * HD),
                                   ACT.Square, scale=r1[:, m:m + 1]).then_inc(evac_done, 1)
                for m in range(M):
                    act.activation(qkv[:, (par * M + m) * QKV:(par * M + m + 1) * QKV], bank(2 * par + m, 0, QKV),
                                   ACT.Copy, scale=r1[:, m:m + 1]).then_inc(evac_done, 1)

            def guess_rsqrt(y, x, x_ready, ln_done, guess, count):
                act.wait_ge(x_ready, count)
                act.activation(y, x, ACT.Ln).then_inc(ln_done, 1)
                act.wait_ge(ln_done, count)
                act.activation(y, y, ACT.Exp, scale=-0.5).then_inc(guess, 1)

            def copy_qkT(f):
                act.wait_ge(tp_done, f)
                act.activation(qkT[:], bank(B_T), ACT.Copy).then_inc(qkT_ready, 1)

            def exps(f, kind):
                act.wait_ge(negmax_done, f)
                for c in range(1 if kind == "fox" else 2):
                    for qb in range(2):
                        lo, n = c * SROW + qb * P, P * (1 + qb)
                        i = 2 * c + qb
                        last = act.activation(s_sb[:, lo:lo + n], s_sb[:, lo:lo + n], ACT.Exp, bias=nmx[:, i:i + 1],
                                              accum_out=lsum[:, i:i + 1])
                last.then_inc(exp_done, 1)

            def copy_pT(f):
                act.wait_ge(pt_done, f)
                act.activation(pT[:], bank(B_T, 0, SROW), ACT.Copy).then_inc(pT_ready, 1)

            def mix_hi(f, kind):
                act.wait_ge(pv_done if kind == "fox" else onorm_done, f)
                src = bank(B_O, 0, S) if kind == "fox" else on[:]
                act.activation(tile(mixed, f - 1, S, 2 * S), src, ACT.Copy).then_inc(mixhi_done, 1)

            def square_o(f):
                act.wait_ge(pv_done, f)
                act.activation(osq[:], bank(B_O, 0, S), ACT.Square).then_inc(osq_done, 1)

            def attention_steps(f, kind, b, at):
                if b == at["turn"]:
                    copy_qkT(f)
                if b == at["scores"]:
                    exps(f, kind)
                if b == at.get("probs"):
                    copy_pT(f)
                if b == at.get("values"):
                    mix_hi(f, kind)

            def trailing_steps(f, b):
                if b == TRAIL_AT["probs"]:
                    copy_pT(f - 1)
                if b == TRAIL_AT["values"]:
                    square_o(f - 1)
                if b == TRAIL_AT["norm"]:
                    guess_rsqrt(org[:], oms[:], ors_in, ors_ln, ors_guess, f - 1)
                if b == TRAIL_AT["norm"] + 1:
                    mix_hi(f - 1, "diff")

            def head_norm(f, kind):
                n = 4 if kind == "fox" else 8
                guess_rsqrt(rsg[:, 0:n], ss2[:, 0:n], rstd_in, rstd_ln, rstd_guess, f)

            def frame(f, par, kind, next_kind, at=None, trail=False, first=False, last=False):
                for b in range(8):
                    if b == 7 and kind is not None:
                        evacuate(f, par)
                    if kind is None and b < 4:
                        x_hi(8 + 2 * b)
                        x_hi(9 + 2 * b)
                        if 4 + b in ACT_SQUARES:
                            x_squares(4 + b)
                    w = PW if last and b >= 4 else W0 if kind is None and b < 4 else W1
                    split_hi(f * 8 + (b + 4), b % RING, f * 2 + (2 + b // 4), w)
                    if b == 7 and kind is None:
                        act.wait_ge(lam_sums, 2)
                        act.activation(lams[:, 2:4], lams[:, 0:2], ACT.Exp).then_inc(lam_exp, 1)
                        guess_rsqrt(r1g[:], rms_in[:], r1_in, r1_ln, r1_guess, 1)
                        act.wait_ge(r1_ready, 1)
                        evacuate(f, par)
                        for m in range(M):
                            act.activation(z[:, m * H:(m + 1) * H], bank(m, QKV, H), ACT.Copy,
                                           scale=r1[:, m:m + 1]).then_inc(z_evac, 1)
                    if b == 7:
                        head_norm(f + 1, next_kind)
                    if kind is not None:
                        attention_steps(f, kind, b, at)
                    if trail:
                        trailing_steps(f, b)
                    if first and b == 1:
                        act.wait_ge(z_abs, 1)
                        act.activation(z[:, 3 * M * H:4 * M * H], z[:, 2 * M * H:3 * M * H], ACT.Exp).then_inc(z_exp, 1)
                        act.wait_ge(z_exp, 1)
                        act.activation(z[:, 4 * M * H:5 * M * H], z[:, 3 * M * H:4 * M * H], ACT.Ln,
                                       bias=1.0).then_inc(z_ln, 1)

            act.preload_act_table_set("natural_log_exp_and_others")
            act.wait_ge(vec_landed, 16)
            for b in range(4):
                x_hi(2 * b)
                x_hi(2 * b + 1)
                split_hi(b, b, 1, W0, free=False)
                if b in ACT_SQUARES:
                    x_squares(b)
            frame(0, 0, None, "diff")
            frame(1, 1, "diff", "diff", DIFF1_AT, first=True)
            with act.Fori(1, H // 2) as i:
                frame(i * 2, 0, "diff", "diff", DIFF_AT, trail=True)
                frame(i * 2 + 1, 1, "diff", "diff", DIFF_AT, trail=True)
            frame(H, 0, "diff", "fox", DIFF_AT, trail=True)
            frame(H + 1, 1, "fox", "fox", FOX1_AT, trail=True)
            with act.Fori(H // 2 + 1, H - 1) as i:
                frame(i * 2, 0, "fox", "fox", FOX_AT)
                frame(i * 2 + 1, 1, "fox", "fox", FOX_AT)
            frame(HEADS - 2, 0, "fox", "fox", FOX_AT)
            frame(HEADS - 1, 1, "fox", "fox", FOX_AT, last=True)

            def x1_parts(n, par, first=False):
                if not first:
                    act.wait_ge(x1sum_done, n - 1)
                act.wait_ge(x1_done, n + 1)
                act.activation(tile(xs, n, S, 2 * S), tile(xT, n), ACT.Copy,
                               scale=tile(vec, n, 1, 1, V_G2)).then_inc(x1hi_done, 1)
                act.activation(sqt[:, par * S:(par + 1) * S], tile(xT, n), ACT.Square).then_inc(x1sq_done, 1)

            for b in range(8):
                split_hi(OUT0 + b + 4, b % RING, OUT0 // RING + 2 + b // 4)
                attention_steps(HEADS, "fox", b, OUT_AT)
            for n in range(4):
                x1_parts(n, n % 2, n < 2)
            with act.Fori(0, (KT - 4) // 2) as i:
                for b in range(4):
                    split_hi(i * 4 + (OUT0 + 8 + b + 4), b, i + (OUT0 // RING + 4))
                    if b % 2:
                        x1_parts(i * 2 + (4 + b // 2), b // 2)

            def conv_tap2(i, gate):
                u, y2, off = (0, 0, 0) if gate else (S + 2, S, 4)
                act.wait_ge(g_u if gate else v_u, i + 1)
                act.activation(y2_t[:, y2:y2 + S], u_t[:, u + 2:u + 2 + S], ACT.Identity,
                               scale=tile(vec, i, 1, 8, V_CW + off + 2), bias=tile(vec, i, 1, 8, V_CW + off + 3)
                               ).then_inc(g_y2 if gate else v_y2, 1)

            def copy_lo(i, b, gate, first):
                if not first:
                    act.wait_ge(g_sum if gate else v_sum, i)
                lo = 0 if gate else S
                act.activation(lo_t[:, lo:lo + S], bank(6 + (not gate), S, S), ACT.Copy).then_inc(g_lo if gate else v_lo, 1)

            def act_hi(i):
                act.wait_ge(a_done, i + 1)
                act.activation(tile(a_s, i, S, 2 * S), a_t[:], ACT.Copy).then_inc(a_hi, 1)

            def up_frame(i, first):
                for b in range(4):
                    if b == 3:
                        act.wait_ge(piece_used, i * 4 + (UP0 + 4))
                        copy_lo(i, b, False, first)
                    split_hi(i * 4 + (UP0 + b + 4), b, i + (UP0 // RING + 2))
                    if b == 0 and not first:
                        conv_tap2(i - 1, False)
                    if b == 1:
                        if first:
                            guess_rsqrt(sqt[:, 0:S], ms2, r2_in, r2_ln, r2_guess, 1)
                        copy_lo(i, b, True, first)
                        if not first:
                            act_hi(i - 1)
                    if b == 2:
                        conv_tap2(i, True)
                    if b == 3:
                        act.wait_ge(g_y, i + 1)
                        if not first:
                            act.wait_ge(a_done, i)
                        act.activation(silu_t[:], y1_t[:, 0:S], ACT.Silu).then_inc(g_silu, 1)

            act.wait_ge(conv_landed, 16)
            up_frame(0, True)
            with act.Fori(1, FT) as i:
                up_frame(i, False)
            for s in range(4):
                split_hi(DOWN0 + s + 4, s, DOWN0 // RING + 2)
                if s == 0:
                    conv_tap2(FT - 1, False)
                if s == 1:
                    act_hi(FT - 1)
            with act.Fori(1, 20) as j:
                for b in range(4):
                    split_hi(j * 4 + (DOWN0 + b + 4), b, j + (DOWN0 // RING + 2))
            for s in (80, 81):
                split_hi(DOWN0 + s + 4, s % RING, (DOWN0 + s + 4) // RING + 1)

        @block.vector
        def _(dve):
            def split_lo(G, s, w=PW):
                dve.wait_ge(hi_ready, G + 1)
                dve.tensor_tensor(slot(w_lo, s, w), slot(raw, s, w), f32(slot(w_hi, s, w)),
                                  ALU.subtract).then_inc(split_done, 1)

            def x_lo(kt):
                dve.wait_ge(xhi_ready, kt + 1)
                c = kt * 2 * S
                dve.scalar_tensor_tensor(out=xs[:, c + S:c + 2 * S], in0=xT[:, kt * S:(kt + 1) * S],
                                         scalar=vec[:, V_G1 + kt:V_G1 + kt + 1], in1=f32(xs[:, c:c + S]),
                                         op0=ALU.mult, op1=ALU.subtract).then_inc(xs_ready, 1)

            def newton(out, x, y, t, guess, count, sq_done, half_done, done):
                dve.wait_ge(guess, count)
                dve.tensor_tensor(t, y, y, ALU.mult).then_inc(sq_done, 1)
                dve.wait_ge(sq_done, count)
                dve.scalar_tensor_tensor(out=t, in0=x, scalar=-0.5, in1=t, op0=ALU.mult, op1=ALU.mult).then_inc(half_done, 1)
                dve.wait_ge(half_done, count)
                dve.scalar_tensor_tensor(out=out, in0=t, scalar=1.5, in1=y, op0=ALU.add, op1=ALU.mult).then_inc(done, 1)

            def norm_qk(f, p, kind):
                n = 4 if kind == "fox" else 8
                w = 2 * M * HD // n
                dve.wait_ge(evac_done, f * 4 - 2)
                dve.tensor_reduce(ss[:, 0:n], sq[:].rearrange("p (n w) -> p n w", w=w), AX_X,
                                  ALU.add).then_inc(sumsq_done, 1)
                dve.wait_ge(sumsq_done, f)
                dve.tensor_scalar(ss2[:, 0:n], ss[:, 0:n], float(w * EPS), None, ALU.add).then_inc(rstd_in, 1)
                newton(rs[:, 0:n], ss2[:, 0:n], rsg[:, 0:n], nt8[:, 0:n], rstd_guess, f, rstd_sq, rstd_half, rstd_done)
                dve.wait_ge(rstd_done, f)
                dve.wait_ge(evac_done, f * 4)
                if kind == "diff":
                    for m in range(M):
                        src = qkv[:, (p * M + m) * QKV:(p * M + m) * QKV + 2 * HD].rearrange("p (n w) -> p n w", w=w)
                        by = rs[:, m * 4:(m + 1) * 4].unsqueeze(2).to_broadcast([P, 4, w])
                        last = dve.tensor_tensor(qn[:, m * 2 * HD:(m + 1) * 2 * HD].rearrange("p (n w) -> p n w", w=w),
                                                 src, by, ALU.mult)
                    last.then_inc(normed, 1)
                    return
                for m in range(M):
                    for j in range(2):
                        src = qkv[:, (p * M + m) * QKV + j * w:(p * M + m) * QKV + (j + 1) * w]
                        i = m * 2 + j
                        last = dve.scalar_tensor_tensor(
                            out=qn[:, m * 2 * HD + j * w:m * 2 * HD + (j + 1) * w], in0=src, scalar=rs[:, i:i + 1],
                            in1=row[:, R_FG + j * w:R_FG + (j + 1) * w], op0=ALU.mult, op1=ALU.mult)
                last.then_inc(normed, 1)

            def row_maxima(f, kind):
                dve.wait_ge(const_landed, 16)
                if kind == "fox":
                    dve.wait_ge(head_bias, f)
                dve.wait_ge(s_done, f)
                n = 2 if kind == "fox" else 4
                for i in range(n):
                    c, lo, w = i // 2, (i % 2) * P, P * (1 + i % 2)
                    add = hbias[:, lo:lo + w] if kind == "fox" else const[:, C_DM + lo:C_DM + lo + w]
                    last = dve.tensor_tensor_reduce(out=s_sb[:, c * SROW + lo:c * SROW + lo + w], in0=bank(B_S + c, lo, w),
                                                    in1=add, scale=1.0, scalar=NEG, op0=ALU.add, op1=ALU.max,
                                                    accum_out=mx[:, i:i + 1])
                last.then_inc(rowmax_done, 1)
                dve.wait_ge(rowmax_done, f)
                dve.tensor_scalar(nmx[:, 0:n], mx[:, 0:n], -1.0, None, ALU.mult).then_inc(negmax_done, 1)

            def normalise(f, kind, first=False):
                dve.wait_ge(exp_done, f)
                n = 2 if kind == "fox" else 4
                dve.reciprocal(rl[:, 0:n], lsum[:, 0:n]).then_inc(recip_done, 1)
                dve.wait_ge(recip_done, f)
                if kind == "fox":
                    for qb in range(2):
                        lo, w = qb * P, P * (1 + qb)
                        last = dve.tensor_scalar(s_sb[:, lo:lo + w], s_sb[:, lo:lo + w], rl[:, qb:qb + 1], None, ALU.mult)
                    last.then_inc(p_ready, 1)
                    return
                if first:
                    dve.wait_ge(lam_ready, 1)
                dve.tensor_scalar(rll[:], rl[:, 2:4], lams[:, 1:2], None, ALU.mult).then_inc(lrecip_done, 1)
                dve.wait_ge(lrecip_done, f)
                for qb in range(2):
                    lo, w = SROW + qb * P, P * (1 + qb)
                    last = dve.tensor_scalar(s_sb[:, lo:lo + w], s_sb[:, lo:lo + w], rll[:, qb:qb + 1], None, ALU.mult)
                last.then_inc(map2_done, 1)
                dve.wait_ge(map2_done, f)
                for qb in range(2):
                    lo, w = qb * P, P * (1 + qb)
                    last = dve.scalar_tensor_tensor(out=pd[:, lo:lo + w], in0=s_sb[:, lo:lo + w], scalar=rl[:, qb:qb + 1],
                                                    in1=s_sb[:, SROW + lo:SROW + lo + w], op0=ALU.mult,
                                                    op1=ALU.subtract)
                last.then_inc(p_ready, 1)

            def mean_square_o(f):
                dve.wait_ge(ors_mm, f)
                dve.tensor_scalar(oms[:], bank(B_O, S, S), EPS, None, ALU.add).then_inc(ors_in, 1)

            def norm_o(f):
                newton(ors[:], oms[:], org[:], osq[:], ors_guess, f, ors_sq, ors_half, ors_done)
                dve.wait_ge(ors_done, f)
                dve.scalar_tensor_tensor(out=on[:], in0=bank(B_O, 0, S), scalar=sg[:], in1=ors[:], op0=ALU.mult,
                                         op1=ALU.mult).then_inc(onorm_done, 1)

            def mix_lo(f, kind):
                dve.wait_ge(mixhi_done, f)
                src = bank(B_O, 0, S) if kind == "fox" else on[:]
                dve.tensor_tensor(tile(mixed, f - 1, S, 2 * S, S), src, f32(tile(mixed, f - 1, S, 2 * S)),
                                  ALU.subtract).then_inc(mixlo_done, 1)

            def forget_bias(h):
                dve.wait_ge(cbc_mm, h + 1)
                for qb in range(2):
                    lo, w = qb * P, P * (1 + qb)
                    last = dve.scalar_tensor_tensor(out=bias[:, h * SROW + lo:h * SROW + lo + w],
                                                    in0=bank(FORGET_BANKS[h], 0, w), scalar=cq[:, qb * H + h:qb * H + h + 1],
                                                    in1=const[:, C_FM + lo:C_FM + lo + w], op0=ALU.subtract,
                                                    op1=ALU.add)
                last.then_inc(bias_built, 1)

            def z_part(i):
                return z[:, i * M * H:(i + 1) * M * H]

            def before_split(f, kind, b, at, trail=False, first=False):
                if trail and b == TRAIL_AT["norm"]:
                    mean_square_o(f - 1)
                if trail and b == TRAIL_AT["norm"] + 2:
                    mix_lo(f - 1, "diff")
                if b == at["scores"]:
                    row_maxima(f, kind)
                if b == at["scores"] + (1 if kind == "fox" else 2):
                    normalise(f, kind, first)

            def after_split(f, kind, b, at, trail=False, first=False):
                if trail and b == TRAIL_AT["norm"]:
                    norm_o(f - 1)
                if b == at.get("values"):
                    mix_lo(f, kind)
                if first and b == 1:
                    dve.wait_ge(z_ln, 1)
                    dve.tensor_tensor(z_part(5), z_part(4), z_part(0), ALU.subtract).then_inc(nlf_ready, 1)
                if first and b == FORGET_AT["sums"]:
                    dve.wait_ge(c_mm, 1)
                    dve.tensor_copy(cT[:], ps[0:H, 0:S])
                    dve.tensor_copy(cq[:], bank(0, S, M * H)).then_inc(c_copied, 1)
                    dve.wait_ge(c_copied, 1)
                for h in range(H):
                    if first and b == FORGET_AT["rows"][h]:
                        forget_bias(h)

            def parameters():
                dve.wait_ge(row_landed, 16)
                dve.tensor_scalar(row[:, R_FG + HD:R_FG + 2 * HD], row[:, R_FG + HD:R_FG + 2 * HD], float(HD) ** 0.5,
                                  None, ALU.mult)
                dve.tensor_scalar(row[:, R_DG + HD:R_DG + 2 * HD], row[:, R_DG + HD:R_DG + 2 * HD], float(DQK) ** 0.5,
                                  None, ALU.mult).then_inc(gains_ready, 1)
                dve.tensor_scalar(sg[:], vec[:, V_SG:V_SG + 1], 1.0 - LAMBDA_INIT, None, ALU.mult)
                for c in range(2):
                    q, k = R_LAM + 2 * c * DQK, R_LAM + (2 * c + 1) * DQK
                    dve.tensor_tensor_reduce(out=lamt[:, c * DQK:(c + 1) * DQK], in0=row[:, q:q + DQK],
                                             in1=row[:, k:k + DQK], scale=1.0, scalar=0.0, op0=ALU.mult, op1=ALU.add,
                                             accum_out=lams[:, c:c + 1]).then_inc(lam_sums, 1)

            def mean_square_x():
                dve.wait_ge(rms1_mm, 1)
                dve.tensor_scalar(rms_in[:, 0:M], bank(B_O, 0, M), EPS, None, ALU.add).then_inc(r1_in, 1)

            def rms_x():
                newton(r1[:], rms_in[:, 0:M], r1g[:], nt1[:], r1_guess, 1, r1_sq, r1_half, r1_ready)

            def lam():
                dve.wait_ge(lam_exp, 1)
                dve.tensor_tensor(lams[:, 0:1], lams[:, 2:3], lams[:, 3:4], ALU.subtract).then_inc(par_step, 1)
                dve.wait_ge(par_step, 1)
                dve.tensor_scalar(lams[:, 1:2], lams[:, 0:1], LAMBDA_INIT, None, ALU.add).then_inc(lam_ready, 1)

            def frame(f, p, kind, next_kind, at=None, trail=False, first=False, last=False):
                if first:
                    lam()
                    dve.wait_ge(z_evac, M)
                    dve.tensor_tensor(z_part(1), z_part(0), row[:, R_BF:R_BF + M * H], ALU.add).then_inc(z_step, 1)
                    dve.wait_ge(z_step, 1)
                    dve.tensor_scalar(z_part(3), z_part(1), -1.0, None, ALU.mult).then_inc(z_step, 1)
                    dve.wait_ge(z_step, 2)
                    dve.tensor_tensor(z_part(2), z_part(1), z_part(3), ALU.min)
                    dve.tensor_scalar(z_part(0), z_part(1), 0.0, None, ALU.min).then_inc(z_abs, 1)
                for b in range(8):
                    if kind is None and b < 4:
                        x_lo(8 + 2 * b)
                        x_lo(9 + 2 * b)
                    w = PW if last and b >= 4 else W0 if kind is None and b < 4 else W1
                    if kind is not None:
                        before_split(f, kind, b, at, trail, first)
                    elif b == 6:
                        parameters()
                    elif b == 7:
                        mean_square_x()
                    if b == 7 and kind is not None:
                        norm_qk(f + 1, 1 - p, next_kind)
                    split_lo(f * 8 + (b + 4), b % RING, w)
                    if b == 7 and kind is None:
                        rms_x()
                        norm_qk(f + 1, 1 - p, next_kind)
                    if kind is not None:
                        after_split(f, kind, b, at, trail, first)

            dve.memset(ones_mean[:], 1.0 / D).then_inc(ones_set, 1)
            dve.memset(ones_sub[:], 1.0 / HD)
            dve.memset(ones_one[:], 1.0)
            dve.memset(u_t[:, 0:2], 0.0)
            dve.memset(u_t[:, S + 2:S + 4], 0.0).then_inc(pad_set, 1)
            for b in range(4):
                if b == 0:
                    dve.wait_ge(vec_landed, 16)
                x_lo(2 * b)
                x_lo(2 * b + 1)
                split_lo(b, b, W0)
            frame(0, 1, None, "diff")
            frame(1, 0, "diff", "diff", DIFF1_AT, first=True)
            with dve.Fori(1, H // 2) as i:
                frame(i * 2, 1, "diff", "diff", DIFF_AT, trail=True)
                frame(i * 2 + 1, 0, "diff", "diff", DIFF_AT, trail=True)
            frame(H, 1, "diff", "fox", DIFF_AT, trail=True)
            frame(H + 1, 0, "fox", "fox", FOX1_AT, trail=True)
            with dve.Fori(H // 2 + 1, H - 1) as i:
                frame(i * 2, 1, "fox", "fox", FOX_AT)
                frame(i * 2 + 1, 0, "fox", "fox", FOX_AT)
            frame(HEADS - 2, 1, "fox", "fox", FOX_AT)
            frame(HEADS - 1, 0, "fox", "fox", FOX_AT, last=True)

            def x1_tile(n, b, par):
                dve.tensor_tensor(xu[:, par * S:(par + 1) * S], bank(b, S, S), tile(xT, n), ALU.add).then_inc(xu_done, 1)
                dve.wait_ge(xu_done, n + 1)
                dve.tensor_tensor(tile(xT, n), bank(b, 0, S), xu[:, par * S:(par + 1) * S], ALU.add).then_inc(x1_done, 1)

            def x1_lo(n):
                dve.wait_ge(x1hi_done, n + 1)
                dve.scalar_tensor_tensor(out=tile(xs, n, S, 2 * S, S), in0=tile(xT, n), scalar=tile(vec, n, 1, 1, V_G2),
                                         in1=f32(tile(xs, n, S, 2 * S)), op0=ALU.mult,
                                         op1=ALU.subtract).then_inc(h2_ready, 1)

            for b in range(8):
                before_split(HEADS, "fox", b, OUT_AT)
                split_lo(OUT0 + b + 4, b % RING)
                after_split(HEADS, "fox", b, OUT_AT)
            dve.wait_ge(piece_used, OUT0 + 8)
            for n in range(4):
                x1_tile(n, n, n % 2)
                if n:
                    x1_lo(n - 1)
            x1_lo(3)
            with dve.Fori(0, (KT - 4) // 2) as i:
                for b in range(4):
                    if b % 2:
                        dve.wait_ge(piece_used, i * 4 + (OUT0 + 8 + b + 1))
                        x1_tile(i * 2 + (4 + b // 2), 4 + b // 2, b // 2)
                    split_lo(i * 4 + (OUT0 + 8 + b + 4), b)
                    if b % 2:
                        x1_lo(i * 2 + (4 + b // 2))

            def sum_halves(i, gate, first):
                off = 0 if gate else S
                dve.wait_ge(g_lo if gate else v_lo, i + 1)
                if not first:
                    dve.wait_ge(g_u if gate else v_u, i)
                dve.tensor_tensor(s_t[:, off:off + S], bank(6 + (not gate), 0, S), lo_t[:, off:off + S],
                                  ALU.add).then_inc(g_sum if gate else v_sum, 1)

            def conv_taps(i, gate):
                u, off, c = (0, 0, 0) if gate else (S + 2, S, 4)
                y, y1 = (y1_t[:, off:off + S], y2_t[:, off:off + S])
                dve.wait_ge(g_y2 if gate else v_y2, i + 1)
                dve.scalar_tensor_tensor(out=y1, in0=u_t[:, u + 1:u + 1 + S], scalar=tile(vec, i, 1, 8, V_CW + c + 1),
                                         in1=y1, op0=ALU.mult, op1=ALU.add).then_inc(g_y1 if gate else v_y1, 1)
                dve.wait_ge(g_y1 if gate else v_y1, i + 1)
                dve.scalar_tensor_tensor(out=y, in0=u_t[:, u:u + S], scalar=tile(vec, i, 1, 8, V_CW + c),
                                         in1=y1, op0=ALU.mult, op1=ALU.add).then_inc(g_y if gate else v_y, 1)

            def gate_times_value(i):
                dve.wait_ge(v_y, i + 1)
                dve.wait_ge(g_silu, i + 1)
                dve.tensor_tensor(a_t[:], silu_t[:], y1_t[:, S:2 * S], ALU.mult).then_inc(a_done, 1)

            def act_lo(i):
                dve.wait_ge(a_hi, i + 1)
                dve.tensor_tensor(tile(a_s, i, S, 2 * S, S), a_t[:], f32(tile(a_s, i, S, 2 * S)),
                                  ALU.subtract).then_inc(a_lo, 1)

            def up_frame(i, first):
                for b in range(4):
                    if b == 3:
                        sum_halves(i, False, first)
                    split_lo(i * 4 + (UP0 + b + 4), b)
                    if b == 0 and not first:
                        conv_taps(i - 1, False)
                        gate_times_value(i - 1)
                    if b == 1:
                        if first:
                            dve.wait_ge(rms2_mm, 1)
                            dve.tensor_scalar(ms2[:], bank(0, 0, S), EPS, None, ALU.add).then_inc(r2_in, 1)
                            newton(r2bc[:], ms2[:], sqt[:, 0:S], sqt[:, S:2 * S], r2_guess, 1, r2_sq, r2_half, r2_ready)
                        sum_halves(i, True, first)
                        if not first:
                            act_lo(i - 1)
                    if b == 2:
                        conv_taps(i, True)

            dve.wait_ge(conv_landed, 16)
            up_frame(0, True)
            with dve.Fori(1, FT) as i:
                up_frame(i, False)
            for s in range(4):
                split_lo(DOWN0 + s + 4, s)
                if s == 0:
                    conv_taps(FT - 1, False)
                    gate_times_value(FT - 1)
                if s == 1:
                    act_lo(FT - 1)

            def out_octet(o):
                partial = [xu[:, 0:S], xu[:, S:2 * S], a_t[:], silu_t[:]]

                def add_second(n):
                    t = OCTET * o + n
                    if n < OCTET - 1:
                        dve.wait_ge(tile_summed, (OCTET - 1) * o + n + 1)
                    else:
                        dve.wait_ge(piece_used, DOWN0 + FT * (o + 1))
                    dve.tensor_tensor(partial[n % 4], bank(n, S, S), xT[:, t * S:(t + 1) * S], ALU.add).then_inc(ou_done, 1)

                def add_first(n):
                    t = OCTET * o + n
                    dve.wait_ge(ou_done, t + 1)
                    dve.tensor_tensor(xT[:, t * S:(t + 1) * S], bank(n, 0, S), partial[n % 4], ALU.add).then_inc(o_done, 1)

                add_second(0)
                for n in range(1, OCTET):
                    add_second(n)
                    add_first(n - 1)
                add_first(OCTET - 1)

            with dve.Fori(1, 10) as j:
                for b in range(4):
                    split_lo(j * 4 + (DOWN0 + b + 4), b)
            split_lo(DOWN0 + 44, 0)
            out_octet(0)
            for s in (45, 46, 47):
                split_lo(DOWN0 + s, s % RING)
            with dve.Fori(11, 20) as j:
                for b in range(4):
                    split_lo(j * 4 + (DOWN0 + b + 4), b)
            for s in (80, 81):
                split_lo(DOWN0 + s + 4, s % RING)
            out_octet(1)

        @block.gpsimd
        def _(pool):
            for i, c in enumerate(SUM_ORDER):
                pool.wait_ge(x_landed[c], 16)
                xc = xT[:, c * XW:(c + 1) * XW]
                if i > 1:
                    pool.wait_ge(xsq_step, 2 * i - 1)
                if c in ACT_SQUARES:
                    pool.wait_ge(xsq_act, ACT_SQUARES.index(c) + 1)
                    pool.tensor_tensor(accx[:, 0:XW], accx[:, 0:XW], sq[:], ALU.add).then_inc(xsq_step, 2)
                    continue
                pool.tensor_tensor(xsq if i else accx[:, 0:XW], xc, xc, ALU.mult).then_inc(xsq_step, 1)
                if i:
                    pool.wait_ge(xsq_step, 2 * i)
                    pool.tensor_tensor(accx[:, 0:XW], accx[:, 0:XW], xsq, ALU.add).then_inc(xsq_step, 1)

            def rotate(f):
                pool.wait_ge(normed, f)
                for m in range(M):
                    qk = qn[:, m * 2 * HD:(m + 1) * 2 * HD]
                    last = pool.tensor_tensor(qk, qk, row[:, R_DG:R_DG + 2 * HD], ALU.mult)
                last.then_inc(gained, 1)
                pool.wait_ge(gained, f)
                q4 = qn[:].rearrange("p (n d) -> p n d", d=DQK)
                x1, x2 = q4[:, :, 0:ROPE_HALF], q4[:, :, ROPE_HALF:2 * ROPE_HALF]
                cos = const[:, C_COS:C_COS + 64].rearrange("p (n d) -> p n d", d=ROPE_HALF)
                sin = const[:, C_SIN:C_SIN + 64].rearrange("p (n d) -> p n d", d=ROPE_HALF)
                t = [rope[:, i * 64:(i + 1) * 64].rearrange("p (n d) -> p n d", d=ROPE_HALF) for i in range(4)]
                pool.tensor_tensor(t[0], x1, cos, ALU.mult)
                pool.tensor_tensor(t[1], x2, sin, ALU.mult)
                pool.tensor_tensor(t[2], x2, cos, ALU.mult)
                pool.tensor_tensor(t[3], x1, sin, ALU.mult).then_inc(rope_prod, 1)
                pool.wait_ge(rope_prod, f)
                pool.tensor_tensor(x1, t[0], t[1], ALU.subtract)
                pool.tensor_tensor(x2, t[2], t[3], ALU.add).then_inc(rope_done, 1)

            pool.wait_ge(const_landed, 16)
            pool.wait_ge(gains_ready, 1)
            with pool.Fori(1, H + 1) as f:
                rotate(f)

            pool.wait_ge(bias_built, 1)
            pool.tensor_copy(hbias[:], bias[:, 0:SROW]).then_inc(head_bias, H + 1)
            with pool.Fori(1, H) as h:
                pool.wait_ge(bias_built, h + 1)
                pool.wait_ge(rowmax_done, h + H)
                pool.tensor_copy(hbias[:], tile(bias, h, SROW, SROW)).then_inc(head_bias, 1)

            for n in range(2):
                pool.wait_ge(x1sq_done, n + 1)
                if n:
                    pool.wait_ge(x1sum_done, n)
                    pool.tensor_tensor(accx[:, 0:S], accx[:, 0:S], sqt[:, S:2 * S], ALU.add).then_inc(x1sum_done, 1)
                else:
                    pool.tensor_copy(accx[:, 0:S], sqt[:, 0:S]).then_inc(x1sum_done, 1)
            with pool.Fori(1, KT // 2) as i:
                for n in range(2):
                    pool.wait_ge(x1sq_done, i * 2 + (n + 1))
                    pool.wait_ge(x1sum_done, i * 2 + n)
                    pool.tensor_tensor(accx[:, 0:S], accx[:, 0:S], sqt[:, n * S:(n + 1) * S], ALU.add).then_inc(x1sum_done, 1)

            pool.wait_ge(pad_set, 1)
            pool.wait_ge(r2_ready, 1)

            def scale_up(i, gate, first):
                off, u = (0, 2) if gate else (S, S + 4)
                pool.wait_ge(g_sum if gate else v_sum, i + 1)
                if not first:
                    pool.wait_ge(g_y if gate else v_y, i)
                pool.tensor_tensor(u_t[:, u:u + S], s_t[:, off:off + S], r2bc[:], ALU.mult).then_inc(g_u if gate else v_u, 1)

            scale_up(0, True, True)
            scale_up(0, False, True)
            with pool.Fori(1, FT) as i:
                scale_up(i, True, False)
                scale_up(i, False, False)


def lay_out(x, norm1_g, w_in, b_forget, fox_q_g, fox_k_g, diff_q_g, diff_k_g, lam_q1, lam_k1, lam_q2, lam_k2,
            diff_subln_g, w_out, norm2_g, w_up, conv_w, conv_b, w_down):
    f = np.ascontiguousarray
    rows = lambda a: a[0].reshape(KT, P, -1)
    w = np.asarray(w_in)[0]
    fw = H * HD
    cut = [w[:, i * fw:(i + 1) * fw] for i in range(3)] + [w[:, 3 * fw + H + i * fw:3 * fw + H + (i + 1) * fw] for i in range(3)]
    flog = w[:, 3 * fw:3 * fw + H]

    def head(j):
        q, k, v = cut[3:6] if j < H else cut[0:3]
        c = slice((j % H) * HD, (j % H + 1) * HD)
        cols = [q[:, c], k[:, c], v[:, c]] + ([flog] if j == 0 else [])
        a = np.concatenate(cols, axis=1)
        return a.reshape(8, 2, P, -1).transpose(0, 2, 1, 3).reshape(8, P, -1)

    win = np.concatenate([head(j) for j in range(1, HEADS)]).reshape(-1, W1)
    wo = np.asarray(w_out)[0].reshape(KT, P, KT, P)
    wo = np.concatenate([wo[H:], wo[:H]])
    out0 = wo[:, :, 0:4].reshape(8, 2, P, 4, P).transpose(0, 2, 1, 3, 4).reshape(8 * P, PW)
    out1 = wo[:, :, 4:].reshape(2, 8, P, KT - 4, P).transpose(3, 0, 2, 1, 4).reshape(-1, PW)
    wu = np.asarray(w_up)[0].reshape(2, 8, P, 2, FT, P)
    up = wu.transpose(4, 3, 0, 2, 1, 5).reshape(-1, PW)
    wd = np.asarray(w_down)[0].reshape(FT, P, 2, PW)
    down = wd.transpose(2, 0, 1, 3).reshape(-1, PW)

    i = np.arange(P)
    tri = (i[:, None] <= i[None, :]).astype(np.float32)
    causal = np.where(i[None, :] <= i[:, None], 0.0, NEG).astype(np.float32)
    chunk = np.where(i[None, :] // CHUNK <= i[:, None] // CHUNK, 0.0, NEG).astype(np.float32)
    zero = np.zeros((P, P), np.float32)
    inv = (np.float32(500000.0) ** (-np.arange(0, 16, 2, dtype=np.float32) / np.float32(16))).astype(np.float32)
    ang = np.arange(S, dtype=np.float32)[:, None] * inv[None, :]
    trig = lambda fn: np.tile(fn(ang).astype(np.float32).reshape(M, P, 1, ROPE_HALF), (1, 1, 4, 1)).transpose(1, 0, 2, 3).reshape(P, -1)
    const = np.concatenate([np.eye(P, dtype=np.float32), tri, np.ones((P, P), np.float32), causal, zero, causal,
                            chunk, zero, chunk, trig(np.cos), trig(np.sin)], axis=1)
    sel = np.repeat(np.eye(H, dtype=np.float32), P, axis=1)

    dq, dk = diff_q_g[0], diff_k_g[0]
    row = np.concatenate([fox_q_g[0], fox_k_g[0], dq, dq, dk, dk, b_forget[0], b_forget[0],
                          lam_q1[0], lam_k1[0], lam_q2[0], lam_k2[0]])[None]
    cw = np.concatenate([np.asarray(conv_w)[0], np.asarray(conv_b)], axis=0)
    cw = cw.reshape(4, 2, FT, P).transpose(3, 2, 1, 0).reshape(P, -1)
    vec = np.concatenate([norm1_g[0].reshape(KT, P).T, norm2_g[0].reshape(KT, P).T, diff_subln_g[0][:, None], cw], axis=1)
    xT = np.asarray(x)[0].T.reshape(KT, P, S).transpose(1, 0, 2).reshape(P, -1)
    return dict(xT=f(xT), w0=f(head(0)), win=f(win), wrest=f(np.concatenate([out0, out1, up, down])), const=f(const),
                sel=f(sel), row=f(row), vec=f(vec))


def kernel(**inputs):
    import concourse.bacc as bacc
    from concourse.bass_utils import run_bass_kernel_spmd

    arrays = lay_out(**{k: np.asarray(v) for k, v in inputs.items()})
    nc = bacc.Bacc("TRN2", target_bir_lowering=False, num_devices=1)
    args = [nc.dram_tensor("in_" + n, a.shape, F32, kind="ExternalInput").ap() for n, a in arrays.items()]
    out = nc.dram_tensor("out", (D, S), F32, kind="ExternalOutput").ap()
    hybrid_layer_kernel(nc, *args, out)
    got = run_bass_kernel_spmd(nc, [{"in_" + n: a for n, a in arrays.items()}], core_ids=[0]).results[0]["out"]
    return np.ascontiguousarray(got.T).reshape(1, S, D)
```
